# Optimizing a Trainium2 kernel written in Bass

```python
import jax
import jax.numpy as jnp
from jax import lax
import numpy as np

D_MODEL = 1024
BATCH = 1
SEQ = 512
DEPTH = 1

HEAD_DIM = 64
A_HEADS = 4
IDX_HEADS = 8
IDX_DIM = 32
DSA_TOPK_MAX = 256
B_HEADS = 4
B_KV_HEADS = 2
WINDOW = 128
C_HEADS = 4
MOBA_BLOCK = 256
MOBA_TOPK = 3
MOBA_Q_CHUNK = 64
D_HEADS = 4
Q_BLOCK = 128
N_BRANCH = 4
BRANCH_WIDTH = 4 * HEAD_DIM
PEER_HEADS = 8
N_KEYS = 128
N_EXPERTS = N_KEYS * N_KEYS
PEER_QDIM = 128
PEER_TOPK = 16
PEER_CHUNK = 128
LN_EPS = 1e-5
NEG_INF = -1e30
DEEPNORM_ALPHA = (2 * DEPTH) ** 0.25
DEEPNORM_BETA = (8 * DEPTH) ** -0.25

IN_WIDTHS = (
    A_HEADS * HEAD_DIM, HEAD_DIM, HEAD_DIM,
    IDX_HEADS * IDX_DIM, IDX_DIM, IDX_HEADS,
    B_HEADS * HEAD_DIM, B_KV_HEADS * HEAD_DIM, B_KV_HEADS * HEAD_DIM,
    C_HEADS * HEAD_DIM, C_HEADS * HEAD_DIM, C_HEADS * HEAD_DIM,
    D_HEADS * HEAD_DIM, D_HEADS * HEAD_DIM, D_HEADS * HEAD_DIM,
    N_BRANCH * D_MODEL,
)
IN_COLS = sum(IN_WIDTHS)
V_COLUMN_GROUPS = (2, 8, 11, 14)

kernel_name = 'hybrid_dsa_swa_moba_stickbreak_peer'

def layer_norm(x, g, b):
    xf = x.astype(jnp.float32)
    mu = jnp.mean(xf, axis=-1, keepdims=True)
    var = jnp.mean(jnp.square(xf - mu), axis=-1, keepdims=True)
    return ((xf - mu) * lax.rsqrt(var + LN_EPS)).astype(g.dtype) * g + b

def alibi_slopes():
    n = A_HEADS + B_HEADS + C_HEADS
    s = 2.0 ** (-8.0 * jnp.arange(1, n + 1, dtype=jnp.float32) / n)
    return s[0::3], s[1::3], s[2::3]

def dsa_attention(q, k, v, q_idx, k_idx, w_idx, slopes):
    bn, s_len = q.shape[:2]
    n_sel = min(DSA_TOPK_MAX, s_len // 4)
    pos_k = jnp.arange(s_len)
    idx_scale = (IDX_DIM * IDX_HEADS) ** -0.5
    k_idx32 = k_idx.astype(jnp.float32)
    k32 = k.astype(jnp.float32)
    v32 = v.astype(jnp.float32)
    gather = jax.vmap(lambda t, ix: t[ix])

    def block(i):
        t0 = i * Q_BLOCK
        pos_q = t0 + jnp.arange(Q_BLOCK)
        qi = lax.dynamic_slice_in_dim(q_idx, t0, Q_BLOCK, 1).astype(jnp.float32)
        wi = lax.dynamic_slice_in_dim(w_idx, t0, Q_BLOCK, 1).astype(jnp.float32)
        qa = lax.dynamic_slice_in_dim(q, t0, Q_BLOCK, 1).astype(jnp.float32)
        rel = jax.nn.relu(jnp.einsum('bqhd,bsd->bqhs', qi, k_idx32))
        score = jnp.einsum('bqhs,bqh->bqs', rel, wi) * idx_scale
        score = jnp.where(pos_k[None, :] <= pos_q[:, None], score, -jnp.inf)
        _, sel = lax.top_k(score, n_sel)
        valid = sel <= pos_q[None, :, None]
        kg = gather(k32, sel)
        vg = gather(v32, sel)
        logits = jnp.einsum('bqhd,bqnd->bhqn', qa, kg) * (HEAD_DIM ** -0.5)
        dist = (pos_q[None, :, None] - sel).astype(jnp.float32)
        logits = logits - slopes[None, :, None, None] * dist[:, None]
        logits = jnp.where(valid[:, None], logits, NEG_INF)
        p = jax.nn.softmax(logits, axis=-1)
        return jnp.einsum('bhqn,bqnd->bqhd', p, vg)

    out = lax.map(block, jnp.arange(s_len // Q_BLOCK))
    return jnp.moveaxis(out, 0, 1).reshape(bn, s_len, A_HEADS * HEAD_DIM)

def swa_sink_attention(q, k, v, sinks, slopes):
    bn, s_len = q.shape[:2]
    w = WINDOW
    nb = s_len // w
    grp = B_HEADS // B_KV_HEADS
    qb = q.astype(jnp.float32).reshape(bn, nb, w, B_KV_HEADS, grp, HEAD_DIM)
    kb = k.astype(jnp.float32).reshape(bn, nb, w, B_KV_HEADS, HEAD_DIM)
    vb = v.astype(jnp.float32).reshape(bn, nb, w, B_KV_HEADS, HEAD_DIM)
    shift = lambda t: jnp.pad(t, ((0, 0), (1, 0), (0, 0), (0, 0), (0, 0)))[:, :-1]
    kk = jnp.concatenate([shift(kb), kb], axis=2)
    vv = jnp.concatenate([shift(vb), vb], axis=2)
    logits = jnp.einsum('bnqkgd,bnskd->bnkgqs', qb, kk) * (HEAD_DIM ** -0.5)
    i = jnp.arange(w)[:, None]
    j = jnp.arange(2 * w)[None, :]
    dist = w + i - j
    band = (dist >= 0) & (dist < WINDOW)
    has_prev = jnp.arange(nb)[:, None, None] > 0
    valid = band[None] & (has_prev | (j >= w)[None])
    sl = slopes.reshape(B_KV_HEADS, grp)[:, :, None, None]
    logits = logits - sl * dist.astype(jnp.float32)
    logits = jnp.where(valid[None, :, None, None], logits, NEG_INF)
    sink = jnp.broadcast_to(sinks.astype(jnp.float32).reshape(B_KV_HEADS, grp, 1, 1), logits.shape[:-1] + (1,))
    p = jax.nn.softmax(jnp.concatenate([logits, sink], axis=-1), axis=-1)[..., :-1]
    o = jnp.einsum('bnkgqs,bnskd->bnqkgd', p, vv)
    return o.reshape(bn, s_len, B_HEADS * HEAD_DIM)

def moba_attention(q, k, v, slopes):
    bn, s_len, nh, hd = q.shape
    nblk = -(-s_len // MOBA_BLOCK)
    s_pad = nblk * MOBA_BLOCK
    n_top = min(MOBA_TOPK, nblk - 1)
    pad = ((0, 0), (0, s_pad - s_len), (0, 0), (0, 0))
    kp = jnp.pad(k.astype(jnp.float32), pad)
    vp = jnp.pad(v.astype(jnp.float32), pad)
    k_blk = kp.reshape(bn, nblk, MOBA_BLOCK, nh, hd).transpose(0, 3, 1, 2, 4)
    v_blk = vp.reshape(bn, nblk, MOBA_BLOCK, nh, hd).transpose(0, 3, 1, 2, 4)
    k_mean = jnp.mean(k_blk, axis=3)
    scale = hd ** -0.5
    offs = jnp.arange(MOBA_BLOCK)
    gather = jax.vmap(jax.vmap(lambda tb, ix: tb[ix]))

    def chunk(i):
        t0 = i * MOBA_Q_CHUNK
        pos_q = t0 + jnp.arange(MOBA_Q_CHUNK)
        own = t0 // MOBA_BLOCK
        qc = lax.dynamic_slice_in_dim(q, t0, MOBA_Q_CHUNK, 1).astype(jnp.float32)
        k_own = lax.dynamic_slice_in_dim(kp, own * MOBA_BLOCK, MOBA_BLOCK, 1)
        v_own = lax.dynamic_slice_in_dim(vp, own * MOBA_BLOCK, MOBA_BLOCK, 1)
        pos_own = own * MOBA_BLOCK + offs
        lo = jnp.einsum('bqhd,bshd->bhqs', qc, k_own) * scale
        lo = lo - slopes[:, None, None] * (pos_q[:, None] - pos_own[None, :]).astype(jnp.float32)
        lo = jnp.where(pos_own[None, :] <= pos_q[:, None], lo, NEG_INF)
        if n_top == 0:
            p_own = jax.nn.softmax(lo, axis=-1)
            return jnp.einsum('bhqs,bshd->bqhd', p_own, v_own)
        gate = jnp.einsum('bqhd,bhnd->bhqn', qc, k_mean)
        gate = jnp.where(jnp.arange(nblk) < own, gate, -jnp.inf)
        _, sel = lax.top_k(gate, n_top)
        ks = gather(k_blk, sel)
        vs = gather(v_blk, sel)
        pos_sel = sel[..., None] * MOBA_BLOCK + offs
        ls = jnp.einsum('bqhd,bhqnsd->bhqns', qc, ks) * scale
        ls = ls - slopes[None, :, None, None, None] * (pos_q[None, None, :, None, None] - pos_sel).astype(jnp.float32)
        ls = jnp.where((sel < own)[..., None], ls, NEG_INF)
        ls = ls.reshape(bn, nh, MOBA_Q_CHUNK, n_top * MOBA_BLOCK)
        p = jax.nn.softmax(jnp.concatenate([ls, lo], axis=-1), axis=-1)
        p_sel = p[..., :n_top * MOBA_BLOCK].reshape(bn, nh, MOBA_Q_CHUNK, n_top, MOBA_BLOCK)
        p_own = p[..., n_top * MOBA_BLOCK:]
        return (jnp.einsum('bhqns,bhqnsd->bqhd', p_sel, vs)
                + jnp.einsum('bhqs,bshd->bqhd', p_own, v_own))

    out = lax.map(chunk, jnp.arange(s_len // MOBA_Q_CHUNK))
    return jnp.moveaxis(out, 0, 1).reshape(bn, s_len, nh * hd)

def stick_breaking_attention(q, k, v):
    bn, s_len, nh, hd = q.shape
    k32 = k.astype(jnp.float32)
    v32 = v.astype(jnp.float32)
    pos_k = jnp.arange(s_len)
    scale = hd ** -0.5

    def block(i):
        t0 = i * Q_BLOCK
        pos_q = t0 + jnp.arange(Q_BLOCK)
        qb = lax.dynamic_slice_in_dim(q, t0, Q_BLOCK, 1).astype(jnp.float32)
        z = jnp.einsum('bqhd,bshd->bhqs', qb, k32) * scale
        strict = pos_k[None, :] < pos_q[:, None]
        log_keep = jnp.where(strict, jax.nn.log_sigmoid(-z), 0.0)
        log_after = lax.cumsum(log_keep, axis=3, reverse=True) - log_keep
        a = jnp.where(strict, jnp.exp(jax.nn.log_sigmoid(z) + log_after), 0.0)
        return jnp.einsum('bhqs,bshd->bqhd', a, v32)

    out = lax.map(block, jnp.arange(s_len // Q_BLOCK))
    return jnp.moveaxis(out, 0, 1).reshape(bn, s_len, nh * hd)

def token_mixer_sublayer(x, w_in, w_branch, w_out, sinks, slopes_a, slopes_b, slopes_c):
    bn, s_len, _ = x.shape
    proj = x @ w_in
    offsets = [int(o) for o in np.cumsum(IN_WIDTHS)[:-1]]
    (qa, ka, va, qi, ki, wi, qb, kb, vb, qc, kc, vc, qd, kd, vd, g) = jnp.split(proj, offsets, axis=-1)
    hd = lambda t, h: t.reshape(bn, s_len, h, HEAD_DIM)
    y_a = dsa_attention(hd(qa, A_HEADS), ka, va, qi.reshape(bn, s_len, IDX_HEADS, IDX_DIM), ki, wi, slopes_a)
    y_b = swa_sink_attention(hd(qb, B_HEADS), hd(kb, B_KV_HEADS), hd(vb, B_KV_HEADS), sinks, slopes_b)
    y_c = moba_attention(hd(qc, C_HEADS), hd(kc, C_HEADS), hd(vc, C_HEADS), slopes_c)
    y_d = stick_breaking_attention(hd(qd, D_HEADS), hd(kd, D_HEADS), hd(vd, D_HEADS))
    ys = jnp.stack([y_a, y_b, y_c, y_d], axis=2)
    branches = jnp.einsum('bsnc,ncd->bsnd', ys, w_branch)
    gates = jax.nn.sigmoid(g.reshape(bn, s_len, N_BRANCH, D_MODEL).astype(jnp.float32))
    merged = jnp.sum(gates * branches, axis=2)
    return merged @ w_out

def peer_ffn(x, wq, subkeys, u, v):
    bn, s_len, d = x.shape
    t_len = bn * s_len
    xt = x.reshape(t_len, d)
    q = (xt @ wq).astype(jnp.float32).reshape(t_len, PEER_HEADS, 2, PEER_QDIM // 2)
    sub = jnp.einsum('thpd,hpkd->thpk', q, subkeys.astype(jnp.float32))
    s_top, i_top = lax.top_k(sub, PEER_TOPK)
    cand = s_top[:, :, 0, :, None] + s_top[:, :, 1, None, :]
    sc, ci = lax.top_k(cand.reshape(t_len, PEER_HEADS, PEER_TOPK * PEER_TOPK), PEER_TOPK)
    i1 = jnp.take_along_axis(i_top[:, :, 0], ci // PEER_TOPK, axis=-1)
    i2 = jnp.take_along_axis(i_top[:, :, 1], ci % PEER_TOPK, axis=-1)
    eid = (i1 * N_KEYS + i2).reshape(t_len, PEER_HEADS * PEER_TOPK)
    gate = jax.nn.softmax(sc, axis=-1).reshape(t_len, PEER_HEADS * PEER_TOPK)
    n_chunks = t_len // PEER_CHUNK

    def chunk(args):
        xc, ec, gc = args
        ug = u[ec]
        h = jax.nn.gelu(jnp.einsum('cd,ced->ce', xc, ug).astype(jnp.float32), approximate=False)
        return jnp.einsum('ce,ced->cd', gc * h, v[ec])

    out = lax.map(chunk, (xt.reshape(n_chunks, PEER_CHUNK, d),
                          eid.reshape(n_chunks, PEER_CHUNK, -1),
                          gate.reshape(n_chunks, PEER_CHUNK, -1)))
    return out.reshape(bn, s_len, d)

def setup_inputs(seed: int = 0) -> dict:
    key = jax.random.key(seed)
    ks = jax.random.split(key, 13)
    nrm = lambda k, shape: jax.random.normal(k, shape, jnp.float32)
    x = nrm(ks[0], (BATCH, SEQ, D_MODEL))
    bounds = np.concatenate([[0], np.cumsum(IN_WIDTHS)])
    col_scale = np.ones((IN_COLS,), np.float32)
    for gi in V_COLUMN_GROUPS:
        col_scale[bounds[gi]:bounds[gi + 1]] = DEEPNORM_BETA
    w_in = nrm(ks[1], (DEPTH, D_MODEL, IN_COLS)) * (D_MODEL ** -0.5) * jnp.asarray(col_scale)
    w_branch = nrm(ks[2], (DEPTH, N_BRANCH, BRANCH_WIDTH, D_MODEL)) * (BRANCH_WIDTH ** -0.5 * DEEPNORM_BETA)
    w_out = nrm(ks[3], (DEPTH, D_MODEL, D_MODEL)) * (D_MODEL ** -0.5 * DEEPNORM_BETA)
    attn_sinks = 0.5 * nrm(ks[4], (DEPTH, B_HEADS))
    ln1_g = 1.0 + 0.02 * nrm(ks[5], (DEPTH, D_MODEL))
    ln1_b = 0.02 * nrm(ks[6], (DEPTH, D_MODEL))
    peer_wq = nrm(ks[7], (DEPTH, D_MODEL, PEER_HEADS * PEER_QDIM)) * (D_MODEL ** -0.5)
    peer_subkeys = nrm(ks[8], (DEPTH, PEER_HEADS, 2, N_KEYS, PEER_QDIM // 2)) * ((PEER_QDIM // 2) ** -0.5)
    peer_u = nrm(ks[9], (DEPTH, N_EXPERTS, D_MODEL)) * (D_MODEL ** -0.5 * DEEPNORM_BETA)
    peer_v = nrm(ks[10], (DEPTH, N_EXPERTS, D_MODEL)) * ((PEER_HEADS * PEER_TOPK) ** -0.5 * DEEPNORM_BETA)
    ln2_g = 1.0 + 0.02 * nrm(ks[11], (DEPTH, D_MODEL))
    ln2_b = 0.02 * nrm(ks[12], (DEPTH, D_MODEL))
    return {'x': x, 'w_in': w_in, 'w_branch': w_branch, 'w_out': w_out, 'attn_sinks': attn_sinks,
            'ln1_g': ln1_g, 'ln1_b': ln1_b, 'peer_wq': peer_wq, 'peer_subkeys': peer_subkeys,
            'peer_u': peer_u, 'peer_v': peer_v, 'ln2_g': ln2_g, 'ln2_b': ln2_b}

def reference(x, w_in, w_branch, w_out, attn_sinks, ln1_g, ln1_b, peer_wq, peer_subkeys,
              peer_u, peer_v, ln2_g, ln2_b):
    slopes_a, slopes_b, slopes_c = alibi_slopes()
    h = x
    for l in range(DEPTH):
        mix = token_mixer_sublayer(h, w_in[l], w_branch[l], w_out[l], attn_sinks[l],
                                   slopes_a, slopes_b, slopes_c)
        h = layer_norm(DEEPNORM_ALPHA * h + mix, ln1_g[l], ln1_b[l])
        ffn = peer_ffn(h, peer_wq[l], peer_subkeys[l], peer_u[l], peer_v[l])
        h = layer_norm(DEEPNORM_ALPHA * h + ffn, ln2_g[l], ln2_b[l])
    return h


_drawn_inputs = setup_inputs


def setup_inputs(seed=0):
    import zlib

    import numpy as np

    out = dict(_drawn_inputs(seed))
    spreads = {}
    factors = {'attn_sinks': 8.0,
     'ln1_g': 2.697,
     'ln1_b': 2.731,
     'peer_wq': 4.89,
     'peer_subkeys': 4.872,
     'peer_u': 5.183,
     'peer_v': 4.875,
     'ln2_g': 2.827,
     'ln2_b': 2.887}
    for name, (base, spread) in spreads.items():
        noise = np.random.default_rng([zlib.crc32(name.encode()), seed]).standard_normal(out[name].shape)
        drawn = base * np.exp(spread * noise) if base else spread * noise
        out[name] = jnp.asarray(drawn.astype(out[name].dtype))
    for name, factor in factors.items():
        out[name] = (out[name] * factor).astype(out[name].dtype)
    return out
```

```python
import concourse.bass as bass
from concourse import mybir

F32 = mybir.dt.float32
F32R = mybir.dt.float32r
U32 = mybir.dt.uint32
ALU = mybir.AluOpType
ACT = mybir.ActivationFunctionType

P = 128
S = 512
NT = S // P
DM = 1024
KC = DM // P
HD = 64
SCALE = HD ** -0.5
NH = 4
IH, ID = 8, 32
IDX_SCALE = (IH * ID) ** -0.5
TOPK = 128
EH, EK = 8, 16
NK = 128
ALPHA = 2.0 ** 0.25
EPS = 1e-5
BIG = 1.0e30
UNSEEN = -2.0e38
TAKEN = -3.0e38
SLOPES = [2.0 ** (-8.0 * i / 12) for i in range(1, 13)]

N_IDX = 4
N_FIRST = 10
N_FILL = 30
N_ATT = N_FIRST + N_FILL
N_GATE_KEPT = 16
N_MERGE = 24
U_OUT = N_ATT + N_MERGE
U_WQ = U_OUT + KC
U_EXP = U_WQ + KC
U_VAL = U_EXP + P
U_END = U_VAL + P
RAW = 4
HI_AHEAD = 3
LO_AHEAD = 2
TOK = 32
NB = S // TOK
ROUTE_UNITS = 12
BANK_EXP = N_ATT + 16

HEADS = [("C", h) for h in range(NH)] + [("D", h) for h in range(NH)] + \
        [("B", h) for h in range(NH)] + [("A", h) for h in range(NH)]
Y_SLOT = {"A": 0, "B": 2, "C": 4, "D": 6}
SET = {"C": 0, "B": 0, "D": 6, "A": 6}
SLOPE = {"A": SLOPES[0::3], "B": SLOPES[1::3], "C": SLOPES[2::3]}
V_CHUNK = {"A": 0, "C": 1, "D": 3, "B": 5}

UNITS = [("proj", s) for s in (6, 7, 8, 9)] + [("proj", s) for s in range(6)] + \
        [("proj", 6 + s) for s in range(6)] + [("gate", g) for g in (0, 1)] + \
        [("proj", s) for s in (0, 1, 2, 3, 4)] + [("gate", g) for g in (2, 3, 4)] + \
        [("proj", s) for s in (6, 7, 8)] + [("gate", g) for g in range(5, 16)]
assert len(UNITS) == N_ATT
V_UNITS = {3: (9, 0), 8: (4, 1), 9: (5, 2), 14: (10, 3), 15: (11, 4), 22: (4, 5)}
MERGE = []
for _c in range(KC):
    if _c >= NH:
        MERGE += [("gate", 4 * _c + _n) for _n in range(4)]
    MERGE.append(("branch", _c))
assert len(MERGE) == N_MERGE


def keys_of(kind, t):
    return (max(t - 1, 0) * P, (1 if t == 0 else 2) * P) if kind == "B" else (0, (t + 1) * P)


def row_at(kind, t):
    return 2 * P * t if kind == "B" else P * t * (t + 1) // 2


def col_at(kt):
    return S * kt - P * kt * (kt - 1) // 2


def transpose_plan():
    order = [("v", 3), ("v", 8), ("v", 9)]
    for u in range(16):
        order += [("u", u, 0), ("u", u, 1)]
        if N_FIRST + 2 * u - 1 in V_UNITS and u > 0:
            order.append(("v", N_FIRST + 2 * u - 1))
        order += [("u", u, 2), ("u", u, 3)]
        if N_FIRST + 2 * u in V_UNITS:
            order.append(("v", N_FIRST + 2 * u))
    read = {"act": 0, "dve": 0}
    plan = {}
    for i, what in enumerate(order):
        by = "dve" if what[0] == "u" and HEADS[what[1]][0] == "D" else "act"
        read[by] += 1
        plan[what] = (i, by, read[by])
        plan[i] = (by, read[by])
    return plan


def peer_block(nc, xT, x_rows, w_units, u_units, v_rows, sinks, ln1_g, ln1_b, subk, ln2_g, ln2_b,
               gelu_d, gate_d, out):
    plan = transpose_plan()
    base = 16512

    def at(name, kb, shape, dt=F32):
        return nc.alloc_sbuf_tensor_at(name, shape, dt, offset=base + int(kb * 1024))

    raw = at("raw", 0, [P, RAW, DM])
    w_hi = at("w_hi", 16, [P, RAW, DM], F32R)
    w_lo = at("w_lo", 32, [P, RAW, DM], F32R)
    tok_hi = at("tok_hi", 48, [P, KC, S], F32R)
    tok_lo = at("tok_lo", 64, [P, KC, S], F32R)
    R = 80
    projT = at("projT", R + 0, [P, 12, S])
    v_tok = at("v_tok", R + 24, [P, 6, NT, P])
    gates = at("gates", R + 36, [P, 16, S])
    y = at("y", R + 68, [P, 8, S])
    x_raw = at("x_raw", R + 68, [P, KC, S])
    row = [at(f"row{i}", R + 84 + 5 * i, [P, 1280]) for i in range(4)]
    colw = at("colw", R + 104, [P, 1280])
    tmp = at("tmp", R + 109, [P, 2, S])
    dist = at("dist", R + 113, [P, S])
    dist_w = at("dist_w", R + 115, [P, 2 * P])
    dist_a = at("dist_a", R + 116, [P, 1280])
    ident = at("ident", R + 121, [P, P])
    neg_after = at("neg_after", R + 121.5, [P, P])
    neg_ones = at("neg_ones", R + 122, [P, P])
    seen = at("seen", R + 122.5, [P, P])
    hide = at("hide", R + 123, [P, P])
    unseen = at("unseen", R + 123.5, [P, P])
    iota = at("iota", R + 124, [P, P])
    small = at("small", R + 124.5, [P, 160])
    mx, nbias, rsum, esink, rinv = (small[:, 8 * i:8 * i + 8].rearrange("p (a t) -> p a t", a=2) for i in range(5))
    top8 = small[:, 40:48]
    sink_t = small[:, 48:52]
    sink8 = small[:, 52:56]
    stats = small[:, 56:104].rearrange("p (t a s) -> p t a s", t=4, a=2)
    mean_var = small[:, 104:112].rearrange("p (t s) -> p t s", t=4)
    var_eps = small[:, 112:116]
    stdev = small[:, 116:120]
    rstd = small[:, 120:124]
    newton = small[:, 124:128]
    y_hi = at("y_hi", R + 0, [P, 8, S], F32R)
    y_lo = at("y_lo", R + 16, [P, 8, S], F32R)
    x_tok = at("x_tok", R + 68, [P, NT, DM])
    m_hi = at("m_hi", R + 84, [P, KC, S], F32R)
    m_lo = at("m_lo", R + 100, [P, KC, S], F32R)
    prod = [at("prod0", R + 32, [P, S]), at("prod1", R + 34, [P, S]),
            at("prod2", R + 116, [P, S]), at("prod3", R + 118, [P, S])]
    ln_g = at("ln_g", R + 0, [P, DM])
    ln_b = at("ln_b", R + 4, [P, DM])
    sk_raw = at("sk_raw", R + 8, [P, EH, 2 * NK])
    sk_hi = at("sk_hi", R + 16, [P, EH, 2 * NK], F32R)
    sk_lo = at("sk_lo", R + 24, [P, EH, 2 * NK], F32R)
    q_hi = at("q_hi", R + 84, [P, EH, S], F32R)
    q_lo = at("q_lo", R + 100, [P, EH, S], F32R)
    sub = at("sub", R + 36, [P, NT, 2 * EH * NK])
    left = at("left", R + 0, [P, 2, 4, P], F32R)
    match = at("match", R + 4, [P, 2, 4, P])
    right_hi = at("right_hi", R + 8, [P, 2, 4, P], F32R)
    right_lo = at("right_lo", R + 12, [P, 2, 4, P], F32R)
    cand = at("cand", R + 16, [P, EH, EK, EK])
    s_top = at("s_top", R + 24, [P, EH, 2, EK])
    i_top = at("i_top", R + 25, [P, EH, 2, EK], U32)
    c_top = at("c_top", R + 26, [P, EH, EK])
    c_pos = at("c_pos", R + 26.5, [P, EH, EK], U32)
    c_row = at("c_row", R + 27, [P, EH * EK], U32)
    c_col = at("c_col", R + 27.5, [P, EH * EK], U32)
    pick = at("pick", R + 28, [P, 3, P])
    i_T = at("i_T", R + 29.5, [P, 2, P])
    g_hi = at("g_hi", R + 30.5, [P, P], F32R)
    g_lo = at("g_lo", R + 31, [P, P], F32R)
    g_sum = at("g_sum", R + 31.5, [P, 2, EH])
    gelu_t = at("gelu_t", R + 32, [P, 2, S])
    stage = [at(f"stage{i}", R + 84 + 16 * i, [P, P, TOK]) for i in range(2)]
    gate_in = [at(f"gate_in{i}", R + 0 + 8 * i, [P, NB, 4, TOK]) for i in range(2)]
    gelu_in = [at(f"gelu_in{i}", R + 16 + 8 * i, [P, 4, S]) for i in range(2)]
    gh = at("gh", R + 60, [P, 2, S])
    gh_hi = at("gh_hi", R + 36, [P, 4, S], F32R)
    gh_lo = at("gh_lo", R + 44, [P, 4, S], F32R)
    ln2_gt = at("ln2_gt", R + 52, [P, DM])
    ln2_bt = at("ln2_bt", R + 56, [P, DM])
    ps = nc.alloc_psum_tensor("ps", [P, 8, S], F32)

    def sem(name):
        return nc.alloc_semaphore(name)

    x_in, const_in, xtok_in, ln_in, sk_in, ln2_in, out_done = (sem(n) for n in (
        "x_in", "const_in", "xtok_in", "ln_in", "sk_in", "ln2_in", "out_done"))
    raw_in = [sem(f"raw_in{i}") for i in range(RAW)]
    hi_done, lo_done, unit_done, bank_read = (sem(n) for n in ("hi_done", "lo_done", "unit_done", "bank_read"))
    x_hi, x_lo, consts, const_step, dve_step, act_step = (sem(n) for n in (
        "x_hi", "x_lo", "consts", "const_step", "dve_step", "act_step"))
    score_full, relu_done, idx_added, score_read = (sem(n) for n in (
        "score_full", "relu_done", "idx_added", "score_read"))
    nbias_set, exp_done, sink_exp, probs_set = (sem(n) for n in ("nbias_set", "exp_done", "sink_exp", "probs_set"))
    abs_set, stick_exp, stick_ln, softplus_set, weight_exp = (sem(n) for n in (
        "abs_set", "stick_exp", "stick_ln", "softplus_set", "weight_exp"))
    tp_full, tp_read_act, tp_read_dve, pv_done, y_set = (sem(n) for n in (
        "tp_full", "tp_read_act", "tp_read_dve", "pv_done", "y_set"))
    y_hi_set, y_lo_set, sig_kept, sig_late, branch_full, merge_step, m_set = (sem(n) for n in (
        "y_hi_set", "y_lo_set", "sig_kept", "sig_late", "branch_full", "merge_step", "m_set"))
    var_set, std_set, h_set, hT_full, hT_hi, hT_lo = (sem(n) for n in (
        "var_set", "std_set", "h_set", "hT_full", "hT_hi", "hT_lo"))
    sk_zero, sk_hi_set, sk_lo_set, q_hi_set, q_lo_set, sub_full, sub_set = (sem(n) for n in (
        "sk_zero", "sk_hi_set", "sk_lo_set", "q_hi_set", "q_lo_set", "sub_full", "sub_set"))
    gelu_out = [sem(f"gelu_out{i}") for i in range(2)]
    route_step, gexp_in, gexp_done, pick_set, pickT_full, pickT_set = (sem(n) for n in (
        "route_step", "gexp_in", "gexp_done", "pick_set", "pickT_full", "pickT_set"))
    gsum_step, route_seen = sem("gsum_step"), sem("route_seen")
    match_set, right_set, right_lo_set, gate_full, gate_read = (sem(n) for n in (
        "match_set", "right_set", "right_lo_set", "gate_full", "gate_read"))
    stage_out = [sem(f"stage_out{i}") for i in range(2)]
    gate_back = [sem(f"gate_back{i}") for i in range(2)]
    gelu_back = [sem(f"gelu_back{i}") for i in range(2)]
    gh_set, gh_hi_set, gh_lo_set, var2_set, std2_set, out_set = (sem(n) for n in (
        "gh_set", "gh_hi_set", "gh_lo_set", "var2_set", "std2_set", "out_set"))

    def score_bank(s):
        return ps[:, 2 + s % 2, :]

    def softmax_index(u):
        return u if u < 4 else u - 4

    def keys_scored(u, i):
        return 3 - i if HEADS[u][0] == "D" else i

    with nc.Block() as block:

        @block.sync
        def _(sp):
            def load_unit(n, src, in_loop=0):
                if n >= RAW:
                    sp.wait_ge(lo_done, in_loop + n - RAW + 1)
                sp.dma_start(raw[:, n % RAW, :], src).then_inc(raw_in[n % RAW], 16)

            sp.dma_start(x_raw[:], xT).then_inc(x_in, 16)
            for n in range(RAW):
                load_unit(n, w_units[n])
            sp.dma_start(sink_t, sinks.to_broadcast([P, NH])).then_inc(const_in, 16)
            for n in range(RAW, U_OUT):
                load_unit(n, w_units[n])
                if n == N_ATT + 5:
                    sp.wait_ge(y_lo_set, 8)
                    sp.dma_start(x_tok[:], x_rows.rearrange("(t p) d -> p t d", p=P)).then_inc(xtok_in, 16)
            for n in range(U_OUT, U_OUT + 4):
                load_unit(n, w_units[n])
            sp.wait_ge(unit_done, U_OUT)
            sp.dma_start(ln_g[:], ln1_g.to_broadcast([P, DM])).then_inc(ln_in, 16)
            sp.dma_start(ln_b[:], ln1_b.to_broadcast([P, DM])).then_inc(ln_in, 16)
            sp.wait_ge(sk_zero, 1)
            for half in range(2):
                sp.dma_start(sk_raw[HD * half:HD * half + HD, :, NK * half:NK * half + NK],
                             subk[half]).then_inc(sk_in, 16)
            for n in range(U_OUT + 4, U_EXP):
                load_unit(n, w_units[n])
            with sp.Fori(0, P // RAW) as i:
                for k in range(RAW):
                    load_unit(U_EXP + k, u_units[bass.ds(RAW * i + k, 1)].rearrange("a p n -> p (a n)"), RAW * i)

            def load_gates(m, slot, read):
                if read is not None:
                    sp.wait_ge(gh_set, read)
                for s in range(2):
                    sp.wait_ge(gelu_out[s], 32 * m + 32)
                sp.dma_start(gate_in[slot][:], gate_d[:, :, bass.ds(4 * m, 4), :].rearrange("b p j t -> p b j t"))\
                    .then_inc(gate_back[slot], 16)
                sp.dma_start(gelu_in[slot][:], gelu_d[bass.ds(4 * m, 4)].rearrange("j p t -> p j t"))\
                    .then_inc(gelu_back[slot], 16)

            def load_values(m):
                for k in range(RAW):
                    load_unit(U_VAL + k, v_rows[:, bass.ds(4 * m + k, 1), :].rearrange("p a d -> p (a d)"), 4 * m)

            sp.wait_ge(gate_read, 2 + P)
            for s in range(2):
                sp.wait_ge(stage_out[s], 16 * (NB // 2 + 1))
            load_gates(0, 0, None)
            load_values(0)
            load_gates(1, 1, None)
            load_values(1)
            sp.dma_start(ln2_gt[:], ln2_g.to_broadcast([P, DM])).then_inc(ln2_in, 16)
            sp.dma_start(ln2_bt[:], ln2_b.to_broadcast([P, DM])).then_inc(ln2_in, 16)
            with sp.Fori(1, P // 8) as i:
                for half in range(2):
                    m = 2 * i + half
                    load_gates(m, half, 4 * m - 4)
                    load_values(m)
            for t in range(NT):
                sp.wait_ge(out_set, t + 1)
                sp.dma_start(out[t * P:(t + 1) * P, :], x_tok[:, t, :]).then_inc(out_done, 16)
            sp.wait_ge(out_done, 16 * NT)

        @block.gpsimd
        def _(pool):
            step = [0]

            def link(ins):
                step[0] += 1
                ins.then_inc(const_step, 1)
                pool.wait_ge(const_step, step[0])

            def select(t, op, fill, base, pattern, mult):
                link(pool.affine_select(out=t, in_=t, compare_op=op, fill=fill, base=base, pattern=pattern,
                                        channel_multiplier=mult))

            def split_lo(n, in_loop=0):
                pool.wait_ge(hi_done, in_loop + n + 1)
                pool.tensor_tensor(w_lo[:, n % RAW, :], raw[:, n % RAW, :], w_hi[:, n % RAW, :].bitcast(F32),
                                   ALU.subtract).then_inc(lo_done, 1)

            exact = dict(allow_small_or_imprecise_dtypes=True)
            link(pool.memset(ident[:], 0.0))
            select(ident[:], ALU.not_equal, 1.0, 0, [[-1, P]], 1)
            split_lo(0)
            link(pool.iota(dist[:], pattern=[[-1, S]], base=S - P, channel_multiplier=1, **exact))
            select(dist[:], ALU.is_ge, BIG, S - P, [[-1, S]], 1)
            link(pool.memset(unseen[:], 0.0))
            select(unseen[:], ALU.is_ge, UNSEEN, 0, [[-1, P]], 1)
            split_lo(1)
            link(pool.iota(dist_w[:], pattern=[[-1, 2 * P]], base=P, channel_multiplier=1, **exact))
            select(dist_w[:], ALU.is_ge, BIG, P, [[-1, 2 * P]], 1)
            select(dist_w[:], ALU.is_gt, BIG, 0, [[1, 2 * P]], -1)
            split_lo(2)
            link(pool.memset(seen[:], 1.0))
            select(seen[:], ALU.is_gt, 0.0, 0, [[1, P]], -1)
            link(pool.memset(hide[:], 0.0))
            select(hide[:], ALU.is_gt, -BIG, 0, [[1, P]], -1)
            split_lo(3)
            link(pool.memset(neg_after[:], -1.0))
            select(neg_after[:], ALU.is_gt, 0.0, 0, [[-1, P]], 1)
            link(pool.memset(neg_ones[:], -1.0))
            pool.iota(iota[:], pattern=[[1, P]], base=0, channel_multiplier=0, **exact).then_inc(consts, 1)
            for n in range(4, U_EXP + LO_AHEAD):
                if n == U_WQ:
                    pool.wait_ge(sk_hi_set, 1)
                    pool.tensor_tensor(sk_lo[:], sk_raw[:], sk_hi[:].bitcast(F32), ALU.subtract)\
                        .then_inc(sk_lo_set, 1)
                if n == U_OUT + 4:
                    pool.wait_ge(unit_done, U_OUT)
                    pool.memset(sk_raw[:], 0.0).then_inc(sk_zero, 1)
                split_lo(n)

            def plain(count, first, in_loop):
                for k in range(count):
                    split_lo(first + k + LO_AHEAD, in_loop)

            with pool.Fori(0, ROUTE_UNITS // 4) as i:
                plain(4, U_EXP, 4 * i)
            with pool.Fori(0, NT) as b:
                plain(8, U_EXP + ROUTE_UNITS, 28 * b)
                with pool.Fori(0, 2) as i:
                    for body in range(2):
                        for k in range(4):
                            split_lo(U_EXP + ROUTE_UNITS + 8 + 4 * body + k + LO_AHEAD, 28 * b + 8 * i)
                            for quad in (2 * k, 2 * k + 1):
                                q = 32 * b + 16 * i + 8 * body + quad
                                pool.wait_ge(match_set, q + 1)
                                pool.tensor_tensor(
                                    right_lo[:, quad % 2], match[:, quad % 2],
                                    g_lo[:, bass.ds(64 * i + 32 * body + 4 * quad, 4)].bitcast(F32)
                                    .unsqueeze(2).to_broadcast([P, 4, P]), ALU.mult).then_inc(right_lo_set, 1)
                plain(4, U_EXP + ROUTE_UNITS + 24, 28 * b)
            plain(4, U_EXP + 124, 0)
            with pool.Fori(0, (P - 4) // 4) as i:
                plain(4, U_VAL, 4 * i)
            for k in range(4 - LO_AHEAD):
                split_lo(U_END - 4 + LO_AHEAD + k)

        @block.scalar
        def _(act):
            def split_hi(n, in_loop=0):
                act.wait_ge(raw_in[n % RAW], 4 * in_loop + 16 * (n // RAW + 1))
                if n >= RAW:
                    act.wait_ge(unit_done, in_loop + n - RAW + 1)
                act.activation(w_hi[:, n % RAW, :], raw[:, n % RAW, :], ACT.Copy).then_inc(hi_done, 1)

            def projected(n):
                kind, k = UNITS[n]
                act.wait_ge(unit_done, n + 1)
                act.activation(projT[:, k, :] if kind == "proj" else gates[:, k, :], ps[:, n % 2, :], ACT.Copy)\
                    .then_inc(bank_read, 1)

            def v_to_tokens(n):
                i = plan["v", n][0]
                act.wait_ge(tp_full, i + 1)
                act.activation(v_tok[:, V_UNITS[n][1]], ps[:, 4 + i % 2, :].rearrange("p (t c) -> p t c", t=NT),
                               ACT.Copy).then_inc(tp_read_act, 1)

            def relu_scores(first):
                for s in range(first, first + 4):
                    act.wait_ge(score_full, s + 1)
                    if s >= 2:
                        act.wait_ge(idx_added, s - 1)
                    n = (s // IH + 2) * P
                    act.activation(tmp[:, s % 2, :n], score_bank(s)[:, :n], ACT.Relu, scale=IDX_SCALE)\
                        .then_inc(relu_done, 1)

            def exponents(u, half):
                kind, h = HEADS[u]
                if kind != "D":
                    su = softmax_index(u)
                    act.wait_ge(nbias_set, 2 * su + half + 1)
                    for t in (2 * half, 2 * half + 1):
                        n, o = keys_of(kind, t)[1], row_at(kind, t)
                        act.activation(row[u % 2][:, o:o + n], row[u % 2][:, o:o + n], ACT.Exp, scale=SCALE,
                                       bias=nbias[:, u % 2, t:t + 1], accum_out=rsum[:, u % 2, t:t + 1])\
                            .then_inc(exp_done, 1)
                        if kind == "B":
                            act.activation(esink[:, u % 2, t:t + 1], sink_t[:, h:h + 1], ACT.Exp,
                                           bias=nbias[:, u % 2, t:t + 1]).then_inc(sink_exp, 1)
                else:
                    d = 4 * (u - 4) + 2 * half
                    for i in range(2):
                        kt = keys_scored(u, 2 * half + i)
                        o, n = col_at(kt), S - kt * P
                        act.wait_ge(abs_set, d + i + 1)
                        act.activation(row[2 + u % 2][:, o:o + n], row[2 + u % 2][:, o:o + n], ACT.Exp)\
                            .then_inc(stick_exp, 1)
                    for i in range(2):
                        kt = keys_scored(u, 2 * half + i)
                        o, n = col_at(kt), S - kt * P
                        act.wait_ge(stick_exp, d + i + 1)
                        act.activation(row[2 + u % 2][:, o:o + n], row[2 + u % 2][:, o:o + n], ACT.Ln, bias=1.0)\
                            .then_inc(stick_ln, 1)

            def weights(u, half):
                kind, _ = HEADS[u]
                for i in (2 * half, 2 * half + 1):
                    idx, _by, _n = plan["u", u, i]
                    if kind != "D":
                        n = (S - i * P) if kind != "B" else min(2, NT - i) * P
                        act.wait_ge(tp_full, idx + 1)
                        act.activation(colw[:, col_at(i):col_at(i) + n], ps[:, 4 + idx % 2, i * P:i * P + n],
                                       ACT.Copy).then_inc(tp_read_act, 1)
                    else:
                        kt = keys_scored(u, i)
                        o, n = col_at(kt), S - kt * P
                        act.wait_ge(tp_read_dve, _n)
                        act.activation(colw[:, o:o + n], colw[:, o:o + n], ACT.Exp).then_inc(weight_exp, 1)

            def unit(n):
                if n + HI_AHEAD < U_END:
                    split_hi(n + HI_AHEAD)
                projected(n)

            act.preload_act_table_set("natural_log_exp_and_others")
            act.wait_ge(x_in, 16)
            for c in range(0, KC, 2):
                act.activation(tok_hi[:, c:c + 2, :], x_raw[:, c:c + 2, :], ACT.Copy).then_inc(x_hi, 1)
                if c // 2 < HI_AHEAD:
                    split_hi(c // 2)
            act.wait_ge(const_in, 16)
            for n in range(N_FIRST):
                unit(n)
                if n == 4:
                    v_to_tokens(3)
                if n >= 4:
                    relu_scores(4 * (n - 4))
            v_to_tokens(8)
            v_to_tokens(9)
            for u in range(-1, 16):
                for half in range(2):
                    n = N_FIRST + 2 * u + half
                    if u + 1 < 16:
                        exponents(u + 1, half)
                    if u >= 0:
                        weights(u, half)
                        if n - 1 in V_UNITS and n - 1 >= N_FIRST:
                            v_to_tokens(n - 1)
                        if n < N_ATT:
                            unit(n)

            act.wait_ge(pv_done, 16)
            for p in range(8):
                act.wait_ge(y_set, p + 1)
                s = Y_SLOT[HEADS[2 * p][0]] + p % 2
                act.activation(y_hi[:, s, :], y[:, s, :], ACT.Copy).then_inc(y_hi_set, 1)
            late = 0
            for k, (kind, c) in enumerate(MERGE):
                n = N_ATT + k
                if k == 0:
                    act.activation(gates[:, 0:4, :], gates[:, 0:4, :], ACT.Sigmoid).then_inc(sig_kept, 1)
                split_hi(n + HI_AHEAD)
                if kind == "gate":
                    act.wait_ge(unit_done, n + 1)
                    act.wait_ge(merge_step, 4 * (c // 4 - NH) + 1)
                    act.activation(gates[:, c - 16, :], ps[:, late % 2, :], ACT.Sigmoid).then_inc(bank_read, 1)
                    late += 1
                elif c + 1 < NH:
                    act.activation(gates[:, 4 * c + 4:4 * c + 8, :], gates[:, 4 * c + 4:4 * c + 8, :], ACT.Sigmoid)\
                        .then_inc(sig_kept, 1)
            for n in range(U_OUT, U_WQ):
                split_hi(n + HI_AHEAD)
                if n == U_OUT + 4:
                    act.wait_ge(sk_in, 32)
                    act.activation(sk_hi[:], sk_raw[:], ACT.Copy).then_inc(sk_hi_set, 1)
            act.wait_ge(var_set, 1)
            act.activation(stdev, var_eps, ACT.Sqrt).then_inc(std_set, 1)
            for t in range(NT):
                act.wait_ge(hT_full, t + 1)
                b = 2 * (t % 2)
                act.activation(tok_hi[:, :, t * P:(t + 1) * P],
                               ps[:, b:b + 2, :].rearrange("p a (c q) -> p (a c) q", c=4), ACT.Copy)\
                    .then_inc(hT_hi, 1)
            for h in range(EH):
                n = U_WQ + h
                split_hi(n + HI_AHEAD)
                act.wait_ge(unit_done, n + 1)
                act.activation(q_hi[:, h, :], ps[:, h % 2, :], ACT.Copy).then_inc(q_hi_set, 1)
            for f in range(16):
                act.wait_ge(sub_full, f + 1)
                act.activation(sub[:, f // 4, S * (f % 4):S * (f % 4) + S], ps[:, 2 + f % 4, :], ACT.Copy)\
                    .then_inc(sub_set, 1)

            def expert_unit(j, in_loop, first=False):
                n = U_EXP + j
                split_hi(n + HI_AHEAD, in_loop)
                act.wait_ge(unit_done, in_loop + n + 1)
                if not first or j >= 2:
                    act.wait_ge(gelu_out[j % 2], 8 * in_loop + 16 * (j // 2))
                act.activation(gelu_t[:, j % 2, :], ps[:, j % 2, :], ACT.Gelu).then_inc(bank_read, 1)
                act.wait_ge(bank_read, in_loop + BANK_EXP + j + 1)
                act.dma_start(gelu_d[bass.ds(in_loop + j, 1)].rearrange("a p t -> p (a t)"), gelu_t[:, j % 2, :])\
                    .then_inc(gelu_out[j % 2], 16)

            act.sem_inc(gate_read, 2)
            for s in range(2):
                act.sem_inc(stage_out[s], 16)
            for k in range(4):
                expert_unit(k, 0, first=True)
            with act.Fori(0, ROUTE_UNITS // 4 - 1) as i:
                for k in range(4):
                    expert_unit(4 + k, 4 * i)
            with act.Fori(0, NT) as b:
                for k in range(4):
                    expert_unit(ROUTE_UNITS + k, 28 * b)
                act.wait_ge(gexp_in, b + 1)
                act.activation(pick[:, 2, :], pick[:, 2, :], ACT.Exp).then_inc(gexp_done, 1)
                for k in range(4, 8):
                    expert_unit(ROUTE_UNITS + k, 28 * b)
                with act.Fori(0, 2) as i:
                    for body in range(2):
                        for k in range(4):
                            expert_unit(ROUTE_UNITS + 8 + 4 * body + k, 28 * b + 8 * i)
                            if k == 0:
                                act.wait_ge(stage_out[body], 32 * b + 16 * i + 16)
                            for quad in (2 * k, 2 * k + 1):
                                q = 32 * b + 16 * i + 8 * body + quad
                                act.wait_ge(gate_full, q + 3)
                                act.activation(
                                    stage[body][:, :, 4 * quad:4 * quad + 4].rearrange("p j t -> p t j"),
                                    ps[:, 2 + quad % 2, :].rearrange("p (t j) -> p t j", t=4), ACT.Copy)\
                                    .then_inc(gate_read, 1)
                        act.wait_ge(gate_read, 32 * b + 16 * i + 8 * body + 8 + 2)
                        act.dma_start(gate_d[bass.ds(4 * b + 2 * i + body, 1)].rearrange("a p j t -> p (a j t)"),
                                      stage[body][:].rearrange("p j t -> p (j t)")).then_inc(stage_out[body], 16)
                for k in range(4):
                    expert_unit(ROUTE_UNITS + 24 + k, 28 * b)
            for k in range(4):
                expert_unit(124 + k, 0)

            def gh_high(j, in_loop):
                act.wait_ge(gh_set, in_loop + j + 1)
                act.wait_ge(unit_done, in_loop + U_VAL + j - 3)
                act.activation(gh_hi[:, j % 4, :], gh[:, j % 2, :], ACT.Copy).then_inc(gh_hi_set, 1)

            gh_high(0, 0)
            gh_high(1, 0)
            with act.Fori(0, (P - 4) // 4) as i:
                for k in range(4):
                    split_hi(U_VAL + k + HI_AHEAD, 4 * i)
                    gh_high(k + 2, 4 * i)
            split_hi(U_END - 1)
            for j in (P - 2, P - 1):
                gh_high(j, 0)
            act.wait_ge(var2_set, 1)
            act.activation(stdev, var_eps, ACT.Sqrt).then_inc(std2_set, 1)

        @block.vector
        def _(dve):
            step = [0]

            def link(ins):
                step[0] += 1
                ins.then_inc(dve_step, 1)
                dve.wait_ge(dve_step, step[0])

            for c in range(0, KC, 2):
                dve.wait_ge(x_hi, c // 2 + 1)
                dve.tensor_tensor(tok_lo[:, c:c + 2, :], x_raw[:, c:c + 2, :], tok_hi[:, c:c + 2, :].bitcast(F32),
                                  ALU.subtract).then_inc(x_lo, 1)
            dve.wait_ge(const_in, 16)
            link(dve.tensor_scalar(sink8, sink_t, 1.0 / SCALE, None, ALU.mult))
            dve.wait_ge(consts, 1)
            link(dve.tensor_copy(dist_a[:, 0:P], dist[:, S - P:S]))

            dve.wait_ge(tp_read_act, 1)
            for s in range(3 * IH):
                t, h = s // IH + 1, s % IH
                n, o = (t + 1) * P, row_at("A", t)
                w = v_tok[:, 0, t, HD + h:HD + h + 1]
                dve.wait_ge(relu_done, s + 1)
                acc = dist_a[:, o:o + n]
                if h == 0:
                    ins = dve.tensor_scalar(acc, tmp[:, s % 2, :n], w, None, ALU.mult)
                else:
                    ins = dve.scalar_tensor_tensor(acc, tmp[:, s % 2, :n], w, acc, ALU.mult, ALU.add)
                ins.then_inc(idx_added, 1)
                dve.wait_ge(idx_added, s + 1)
                if h == IH - 1:
                    link(dve.tensor_tensor(dist_a[:, o + n - P:o + n], dist_a[:, o + n - P:o + n], unseen[:], ALU.add))

            def choose_keys(r):
                t = r // (TOPK // 8) + 1
                n, o = (t + 1) * P, row_at("A", t)
                left_over = dist_a[:, o:o + n]
                link(dve.max(top8, left_over))
                link(dve.match_replace(left_over, top8, left_over, TAKEN))
                if r % (TOPK // 8) == TOPK // 8 - 1:
                    link(dve.tensor_scalar(left_over, left_over, 0.5 * (TAKEN + UNSEEN), BIG, ALU.is_gt, ALU.mult))
                    link(dve.tensor_tensor(left_over, left_over, dist[:, S - n:S], ALU.add))

            def scores(u, half):
                kind, h = HEADS[u]
                s0 = 24 + 4 * u + 2 * half
                if kind != "D":
                    su = softmax_index(u)
                    src = {"A": dist_a[:], "B": dist_w[:], "C": dist[:]}[kind]
                    width = {"A": 1280, "B": 2 * P, "C": S}[kind]
                    bias = row[2][:, :width]
                    if half == 0:
                        link(dve.tensor_scalar(bias, src, -SLOPE[kind][h] / SCALE, None, ALU.mult))
                    for i in range(2):
                        t = 2 * half + i
                        n, o = keys_of(kind, t)[1], row_at(kind, t)
                        b = bias[:, o:o + n] if kind == "A" else bias[:, width - n:width]
                        dve.wait_ge(score_full, s0 + i + 1)
                        dve.tensor_tensor_reduce(
                            out=row[u % 2][:, o:o + n], in0=score_bank(s0 + i)[:, :n], in1=b, scale=1.0,
                            scalar=-3.0e38, op0=ALU.add, op1=ALU.max, accum_out=mx[:, u % 2, t:t + 1])\
                            .then_inc(score_read, 1)
                    dve.wait_ge(score_read, 4 * u + 2 * half + 2)
                    two = slice(2 * half, 2 * half + 2)
                    if kind == "B":
                        ins = dve.tensor_scalar(nbias[:, u % 2, two], mx[:, u % 2, two], sink8[:, h:h + 1], -SCALE,
                                                ALU.max, ALU.mult)
                    else:
                        ins = dve.tensor_scalar(nbias[:, u % 2, two], mx[:, u % 2, two], -SCALE, None, ALU.mult)
                    ins.then_inc(nbias_set, 1)
                else:
                    d = 4 * (u - 4) + 2 * half
                    for i in range(2):
                        kt = keys_scored(u, 2 * half + i)
                        o, n = col_at(kt), S - kt * P
                        dve.wait_ge(score_full, s0 + i + 1)
                        dve.tensor_scalar(tmp[:, i, :n], score_bank(s0 + i)[:, :n], SCALE, None, ALU.mult)\
                            .then_inc(score_read, 1)
                        dve.wait_ge(score_read, 4 * u + 2 * half + i + 1)
                        dve.scalar_tensor_tensor(row[2 + u % 2][:, o:o + n], tmp[:, i, :n], -1.0, tmp[:, i, :n],
                                                 ALU.mult, ALU.min).then_inc(abs_set, 1)

            def scores_end(u, half):
                kind, h = HEADS[u]
                if kind != "D":
                    su = softmax_index(u)
                    two = slice(2 * half, 2 * half + 2)
                    dve.wait_ge(exp_done, 4 * su + 2 * half + 2)
                    if kind == "B":
                        dve.wait_ge(sink_exp, 4 * h + 2 * half + 2)
                        link(dve.tensor_tensor(rsum[:, u % 2, two], rsum[:, u % 2, two], esink[:, u % 2, two], ALU.add))
                    link(dve.reciprocal(rinv[:, u % 2, two], rsum[:, u % 2, two]))
                    for t in (2 * half, 2 * half + 1):
                        n, o = keys_of(kind, t)[1], row_at(kind, t)
                        dve.tensor_scalar(row[u % 2][:, o:o + n], row[u % 2][:, o:o + n], rinv[:, u % 2, t:t + 1],
                                          None, ALU.mult).then_inc(probs_set, 1)
                else:
                    d = 4 * (u - 4) + 2 * half
                    for i in range(2):
                        kt = keys_scored(u, 2 * half + i)
                        o, n = col_at(kt), S - kt * P
                        sp_, ls = row[u % 2], row[2 + u % 2]
                        dve.wait_ge(stick_ln, d + i + 1)
                        link(dve.scalar_tensor_tensor(sp_[:, o:o + n], tmp[:, i, :n], 0.0, ls[:, o:o + n],
                                                      ALU.max, ALU.add))
                        dve.tensor_tensor(sp_[:, o:o + P], sp_[:, o:o + P], seen[:], ALU.mult)\
                            .then_inc(softplus_set, 1)
                        link(dve.scalar_tensor_tensor(ls[:, o:o + n], tmp[:, i, :n], 0.0, ls[:, o:o + n],
                                                      ALU.min, ALU.subtract))
                        link(dve.tensor_tensor(ls[:, o:o + P], ls[:, o:o + P], hide[:], ALU.add))

            def weights(u, half):
                if HEADS[u][0] != "D":
                    return
                for i in (2 * half, 2 * half + 1):
                    kt = keys_scored(u, i)
                    o, n = col_at(kt), S - kt * P
                    idx = plan["u", u, i][0]
                    dve.wait_ge(tp_full, idx + 1)
                    dve.tensor_tensor(colw[:, o:o + n], ps[:, 4 + idx % 2, :n], row[2 + u % 2][:, o:o + n],
                                      ALU.add).then_inc(tp_read_dve, 1)

            def store_y(p):
                kind = HEADS[2 * p][0]
                dve.wait_ge(pv_done, 2 * p + 2)
                dve.tensor_copy(y[:, Y_SLOT[kind] + p % 2, :], ps[:, 6 + p % 2, :]).then_inc(y_set, 1)

            r = 0
            for u in range(-1, 16):
                for half in range(2):
                    if u + 1 < 16:
                        scores(u + 1, half)
                    if u >= 0:
                        weights(u, half)
                    if half == 1 and u >= 2 and u % 2 == 0:
                        store_y(u // 2 - 1)
                    if u >= 0:
                        for _ in range(2 + half):
                            if r < 3 * TOPK // 8:
                                choose_keys(r)
                                r += 1
                    if u + 1 < 16:
                        scores_end(u + 1, half)
                assert u < 10 or r == 3 * TOPK // 8
            store_y(7)

            dve.wait_ge(pv_done, 16)
            for p in range(8):
                s = Y_SLOT[HEADS[2 * p][0]] + p % 2
                dve.wait_ge(y_hi_set, p + 1)
                dve.tensor_tensor(y_lo[:, s, :], y[:, s, :], y_hi[:, s, :].bitcast(F32), ALU.subtract)\
                    .then_inc(y_lo_set, 1)
            for c in range(KC):
                for k, n in enumerate((2, 3, 1, 0)):
                    if k < 3:
                        dve.wait_ge(branch_full, 3 * c + k + 1)
                    else:
                        dve.wait_ge(unit_done, N_ATT + MERGE.index(("branch", c)) + 1)
                    if c < NH:
                        dve.wait_ge(sig_kept, c + 1)
                    else:
                        dve.wait_ge(bank_read, N_ATT + 4 * (c - NH) + n + 1)
                    slot = (4 * c + n) % 16
                    dve.tensor_tensor(prod[n][:], ps[:, 2 + n, :], gates[:, slot, :], ALU.mult).then_inc(dve_step, 1)
                    step[0] += 1
                dve.wait_ge(dve_step, step[0])
                dve.tensor_tensor(prod[0][:], prod[0][:], prod[1][:], ALU.add).then_inc(merge_step, 1)
                dve.wait_ge(merge_step, 4 * c + 1)
                dve.tensor_tensor(prod[2][:], prod[2][:], prod[3][:], ALU.add).then_inc(merge_step, 1)
                dve.wait_ge(merge_step, 4 * c + 2)
                dve.tensor_tensor(prod[0][:], prod[0][:], prod[2][:], ALU.add).then_inc(merge_step, 1)
                dve.wait_ge(merge_step, 4 * c + 3)
                dve.tensor_copy(m_hi[:, c, :], prod[0][:]).then_inc(merge_step, 1)
                dve.wait_ge(merge_step, 4 * c + 4)
                dve.tensor_tensor(m_lo[:, c, :], prod[0][:], m_hi[:, c, :].bitcast(F32), ALU.subtract).then_inc(m_set, 1)
                dve.wait_ge(m_set, c + 1)

            def norm(g_tile, b_tile, loaded, full, var_sem, std_sem, done):
                dve.wait_ge(loaded[0], loaded[1])
                dve.wait_ge(unit_done, full)
                for t in range(NT):
                    link(dve.scalar_tensor_tensor(
                        x_tok[:, t, :].rearrange("p (a n) -> p a n", a=2),
                        x_tok[:, t, :].rearrange("p (a n) -> p a n", a=2), ALPHA, ps[:, 2 * t:2 * t + 2, :],
                        ALU.mult, ALU.add))
                    for a in range(2):
                        ins = dve.bn_stats(stats[:, t, a], x_tok[:, t, a * S:a * S + S])
                        step[0] += 1
                        ins.then_inc(dve_step, 1)
                    dve.wait_ge(dve_step, step[0])
                    link(dve.bn_aggr(mean_var[:, t], stats[:, t]))
                dve.tensor_scalar(var_eps, mean_var[:, :, 1], EPS, None, ALU.add).then_inc(var_sem, 1)
                dve.wait_ge(std_sem, 1)
                link(dve.reciprocal(rstd, stdev))
                link(dve.tensor_tensor(newton, rstd, rstd, ALU.mult))
                link(dve.tensor_tensor(newton, newton, var_eps, ALU.mult))
                link(dve.tensor_scalar(newton, newton, -0.5, 1.5, ALU.mult, ALU.add))
                link(dve.tensor_tensor(rstd, rstd, newton, ALU.mult))
                for t in range(NT):
                    link(dve.tensor_scalar(x_tok[:, t, :], x_tok[:, t, :], mean_var[:, t, 0:1], rstd[:, t:t + 1],
                                           ALU.subtract, ALU.mult))
                    link(dve.tensor_tensor(x_tok[:, t, :], x_tok[:, t, :], g_tile[:], ALU.mult))
                    dve.tensor_tensor(x_tok[:, t, :], x_tok[:, t, :], b_tile[:], ALU.add).then_inc(done, 1)

            dve.wait_ge(xtok_in, 16)
            norm(ln_g, ln_b, (ln_in, 32), U_WQ, var_set, std_set, h_set)
            for t in range(NT):
                b = 2 * (t % 2)
                dve.wait_ge(hT_hi, t + 1)
                dve.tensor_tensor(tok_lo[:, :, t * P:(t + 1) * P],
                                  ps[:, b:b + 2, :].rearrange("p a (c q) -> p (a c) q", c=4),
                                  tok_hi[:, :, t * P:(t + 1) * P].bitcast(F32), ALU.subtract).then_inc(hT_lo, 1)
            for h in range(EH):
                dve.wait_ge(q_hi_set, h + 1)
                dve.tensor_tensor(q_lo[:, h, :], ps[:, h % 2, :], q_hi[:, h, :].bitcast(F32), ALU.subtract)\
                    .then_inc(q_lo_set, 1)

            ROUTE_STEPS = 18

            def route(b):
                n_step = [0]

                def settled(ins):
                    n_step[0] += 1
                    ins.then_inc(route_step, 1)
                    dve.wait_ge(route_step, ROUTE_STEPS * b + n_step[0])
                    dve.sem_inc(route_seen, 1)

                halves = [(h, p) for h in range(EH) for p in range(2)]
                work = cand[:].rearrange("p h a c -> p (h a c)").rearrange("p (h s k) -> p h s k", h=EH, s=2)
                settled(dve.tensor_copy(cand[:].rearrange("p h a c -> p (h a c)"),
                                        sub[:, bass.ds(b, 1), :].rearrange("p a n -> p (a n)")))
                for h, p in halves:
                    ins = dve.max(s_top[:, h, p, 0:8], work[:, h, p, :])
                settled(ins)
                for h, p in halves:
                    ins = dve.max_index(i_top[:, h, p, 0:8], s_top[:, h, p, 0:8], work[:, h, p, :])
                settled(ins)
                for h, p in halves:
                    ins = dve.match_replace(work[:, h, p, :], s_top[:, h, p, 0:8], work[:, h, p, :], TAKEN)
                settled(ins)
                for h, p in halves:
                    ins = dve.max(s_top[:, h, p, 8:16], work[:, h, p, :])
                settled(ins)
                for h, p in halves:
                    ins = dve.max_index(i_top[:, h, p, 8:16], s_top[:, h, p, 8:16], work[:, h, p, :])
                settled(ins)
                settled(dve.tensor_tensor(
                    cand[:], s_top[:, :, 0, :].unsqueeze(3).to_broadcast([P, EH, EK, EK]),
                    s_top[:, :, 1, :].unsqueeze(2).to_broadcast([P, EH, EK, EK]), ALU.add))
                rows = cand[:].rearrange("p h a c -> p h (a c)")
                for h in range(EH):
                    ins = dve.max(c_top[:, h, 0:8], rows[:, h, :])
                settled(ins)
                for h in range(EH):
                    ins = dve.max_index(c_pos[:, h, 0:8], c_top[:, h, 0:8], rows[:, h, :])
                settled(ins)
                for h in range(EH):
                    ins = dve.match_replace(rows[:, h, :], c_top[:, h, 0:8], rows[:, h, :], TAKEN)
                settled(ins)
                for h in range(EH):
                    ins = dve.max(c_top[:, h, 8:16], rows[:, h, :])
                settled(ins)
                dve.tensor_tensor(pick[:, 2, :].rearrange("p (h k) -> p h k", h=EH), c_top[:],
                                  c_top[:, :, 0:1].to_broadcast([P, EH, EK]), ALU.subtract).then_inc(gexp_in, 1)
                for h in range(EH):
                    ins = dve.max_index(c_pos[:, h, 8:16], c_top[:, h, 8:16], rows[:, h, :])
                settled(ins)
                pos = c_pos[:].rearrange("p h k -> p (h k)")
                dve.tensor_scalar(c_row[:], pos, 4, None, ALU.logical_shift_right)
                settled(dve.tensor_scalar(c_col[:], pos, EK - 1, None, ALU.bitwise_and))
                for p, rank in ((0, c_row), (1, c_col)):
                    hot = cand[:].rearrange("p h a c -> p (h a) c")
                    settled(dve.tensor_tensor(hot, rank[:].unsqueeze(2).to_broadcast([P, EH * EK, EK]),
                                              iota[:, 0:EK].unsqueeze(1).to_broadcast([P, EH * EK, EK]),
                                              ALU.is_equal))
                    settled(dve.tensor_tensor(cand[:], cand[:],
                                              i_top[:, :, p, :].unsqueeze(2).to_broadcast([P, EH, EK, EK]), ALU.mult))
                    ins = dve.tensor_reduce(pick[:, p, :], hot, mybir.AxisListType.X, ALU.add)
                    if p == 0:
                        settled(ins)
                dve.wait_ge(gexp_done, b + 1)
                g = pick[:, 2, :].rearrange("p (h k) -> p h k", h=EH)
                settled2(dve.tensor_reduce(g_sum[:, 0, :], g, mybir.AxisListType.X, ALU.add), b, 1)
                settled2(dve.reciprocal(g_sum[:, 1, :], g_sum[:, 0, :]), b, 2)
                dve.tensor_tensor(g, g, g_sum[:, 1, :].unsqueeze(2).to_broadcast([P, EH, EK]), ALU.mult)\
                    .then_inc(pick_set, 1)
                assert n_step[0] == ROUTE_STEPS, n_step[0]
                dve.wait_ge(pickT_full, b + 1)
                dve.tensor_copy(i_T[:], ps[:, 4, 0:2 * P].rearrange("p (a t) -> p a t", a=2))
                dve.tensor_copy(g_hi[:], ps[:, 4, 2 * P:3 * P]).then_inc(pickT_set, 1)
                dve.wait_ge(pickT_set, 2 * b + 1)
                dve.tensor_tensor(g_lo[:], ps[:, 4, 2 * P:3 * P], g_hi[:].bitcast(F32), ALU.subtract)\
                    .then_inc(pickT_set, 1)
                dve.wait_ge(pickT_set, 2 * b + 2)
                dve.sem_inc(route_seen, 1)

            def settled2(ins, b, k):
                ins.then_inc(gsum_step, 1)
                dve.wait_ge(gsum_step, 2 * b + k)

            def mark(b, i, body, quad):
                q = 32 * b + 16 * i + 8 * body + quad
                tok = bass.ds(64 * i + 32 * body + 4 * quad, 4)
                keys = iota[:].unsqueeze(1).to_broadcast([P, 4, P])
                s = quad % 2
                dve.wait_ge(gate_full, q + 1)
                dve.tensor_tensor(match[:, s], keys, i_T[:, 1, tok].unsqueeze(2).to_broadcast([P, 4, P]),
                                  ALU.is_equal).then_inc(match_set, 1)
                dve.tensor_tensor(left[:, s], keys, i_T[:, 0, tok].unsqueeze(2).to_broadcast([P, 4, P]),
                                  ALU.is_equal)
                dve.wait_ge(match_set, q + 1)
                dve.tensor_tensor(right_hi[:, s], match[:, s],
                                  g_hi[:, tok].bitcast(F32).unsqueeze(2).to_broadcast([P, 4, P]), ALU.mult)\
                    .then_inc(right_set, 1)

            dve.wait_ge(sub_set, 16)
            with dve.Fori(0, NT) as b:
                route(b)
                with dve.Fori(0, 2) as i:
                    for body in range(2):
                        for quad in range(8):
                            mark(b, i, body, quad)

            def gate_times_gelu(j, k, m, first=False):
                slot = (k // 4) % 2
                if k % 4 == 0:
                    dve.wait_ge(gate_back[slot], m)
                    dve.wait_ge(gelu_back[slot], m)
                dve.tensor_tensor(gh[:, k % 2, :].rearrange("p (b t) -> p b t", b=NB),
                                  gate_in[slot][:, :, k % 4, :],
                                  gelu_in[slot][:, k % 4, :].rearrange("p (b t) -> p b t", b=NB), ALU.mult)\
                    .then_inc(gh_set, 1)
                dve.wait_ge(gh_hi_set, j + 1)
                dve.tensor_tensor(gh_lo[:, k % 4, :], gh[:, k % 2, :], gh_hi[:, k % 4, :].bitcast(F32),
                                  ALU.subtract).then_inc(gh_lo_set, 1)

            with dve.Fori(0, P // 8) as i:
                for k in range(8):
                    gate_times_gelu(8 * i + k, k, 16 * i + 16)
            norm(ln2_gt, ln2_bt, (ln2_in, 32), U_END, var2_set, std2_set, out_set)

        @block.tensor
        def _(pe):
            def three(out_, l_hi, l_lo, r_hi, r_lo, start, stop):
                pe.matmul(out_, l_hi, r_hi, start=start, stop=False)
                pe.matmul(out_, l_hi, r_lo, start=False, stop=False)
                return pe.matmul(out_, l_lo, r_hi, start=False, stop=stop)

            def project(n, bank, in_loop=0):
                pe.wait_ge(lo_done, in_loop + n + 1)
                s = n % RAW
                for c in range(KC):
                    cols = slice(c * P, (c + 1) * P)
                    last = three(ps[:, bank, :], w_hi[:, s, cols], w_lo[:, s, cols], tok_hi[:, c, :], tok_lo[:, c, :],
                                 c == 0, c == KC - 1)
                last.then_inc(unit_done, 1)

            def att_unit(n):
                if n >= 2:
                    pe.wait_ge(bank_read, n - 1)
                project(n, n % 2)

            def tp_bank(what):
                i = plan[what][0]
                if i >= 2:
                    by, n = plan[i - 2]
                    pe.wait_ge(tp_read_act if by == "act" else tp_read_dve, n)
                return ps[:, 4 + i % 2, :]

            def v_to_tokens(n):
                bank = tp_bank(("v", n))
                pe.wait_ge(bank_read, n + 1)
                for t in range(NT):
                    last = pe.transpose(bank[:, t * P:(t + 1) * P], projT[:, V_UNITS[n][0], t * P:(t + 1) * P], ident[:])
                last.then_inc(tp_full, 1)

            def score_free(s):
                if s < 2:
                    return
                if s - 2 < 24:
                    pe.wait_ge(relu_done, s - 1)
                else:
                    pe.wait_ge(score_read, s - 2 - 24 + 1)

            def index_scores(first):
                pe.wait_ge(bank_read, 3)
                for s in range(first, first + 4):
                    t, h = s // IH + 1, s % IH
                    rows = slice(ID * (h % 4), ID * (h % 4) + ID)
                    score_free(s)
                    pe.matmul(score_bank(s)[:, :(t + 1) * P], projT[rows, 6 + h // 4, t * P:(t + 1) * P],
                              projT[rows, 8, :(t + 1) * P], start=True, stop=True).then_inc(score_full, 1)

            def scores(u, half):
                kind, h = HEADS[u]
                pe.wait_ge(bank_read, {"C": 8, "D": 14, "B": 22, "A": 29}[kind])
                rows = slice(HD * (h % 2), HD * (h % 2) + HD)
                q = projT[rows, SET[kind] + h // 2, :]
                k = projT[rows, SET[kind] + 2 + (0 if kind == "A" else h // 2), :]
                for i in (2 * half, 2 * half + 1):
                    s = 24 + 4 * u + i
                    score_free(s)
                    if kind == "D":
                        kt = keys_scored(u, i)
                        pe.matmul(score_bank(s)[:, :S - kt * P], k[:, kt * P:(kt + 1) * P], q[:, kt * P:S],
                                  start=True, stop=True).then_inc(score_full, 1)
                    else:
                        k0, n = keys_of(kind, i)
                        pe.matmul(score_bank(s)[:, :n], q[:, i * P:(i + 1) * P], k[:, k0:k0 + n],
                                  start=True, stop=True).then_inc(score_full, 1)

            def weights(u, half):
                kind, h = HEADS[u]
                for i in (2 * half, 2 * half + 1):
                    bank = tp_bank(("u", u, i))
                    if kind == "D":
                        kt = keys_scored(u, i)
                        pe.wait_ge(softplus_set, 4 * (u - 4) + i + 1)
                        for k2 in range(kt, NT):
                            o, n = col_at(k2), S - k2 * P
                            last = pe.matmul(bank[:, (k2 - kt) * P:S - kt * P], (neg_after if k2 == kt else neg_ones)[:],
                                             row[u % 2][:, o:o + n], start=k2 == kt, stop=k2 == NT - 1)
                    else:
                        pe.wait_ge(probs_set, 4 * softmax_index(u) + 4)
                        for t in range(i, NT if kind != "B" else min(i + 2, NT)):
                            o = row_at(kind, t) + i * P - keys_of(kind, t)[0]
                            last = pe.transpose(bank[:, t * P:(t + 1) * P], row[u % 2][:, o:o + P], ident[:])
                    last.then_inc(tp_full, 1)

            def outputs(u):
                kind, h = HEADS[u]
                rows = slice(HD * (h % 2), HD * (h % 2) + HD)
                bank = ps[rows, 6 + (u // 2) % 2, :]
                if u >= 4 and u % 2 == 0:
                    pe.wait_ge(y_set, u // 2 - 1)
                if kind == "D":
                    pe.wait_ge(weight_exp, 4 * (u - 4) + 4)
                else:
                    pe.wait_ge(tp_read_act, plan["u", u, 3][2])
                chunk = V_CHUNK[kind] + (h // 2 if kind in "CD" else 0)
                c0 = {"A": 0, "B": HD * (h // 2)}.get(kind, HD * (h % 2))
                v = v_tok[:, chunk, :, c0:c0 + HD]
                if kind == "B":
                    for t in range(NT):
                        for kt in range(max(t - 1, 0), t + 1):
                            o = col_at(kt) + (t - kt) * P
                            last = pe.matmul(bank[:, t * P:(t + 1) * P], v[:, kt, :], colw[:, o:o + P],
                                             start=kt == max(t - 1, 0), stop=kt == t)
                else:
                    for kt in range(NT):
                        o, n = col_at(kt), S - kt * P
                        last = pe.matmul(bank[:, kt * P:S], v[:, kt, :], colw[:, o:o + n],
                                         start=kt == 0, stop=kt == NT - 1)
                last.then_inc(pv_done, 1)

            pe.wait_ge(x_lo, 4)
            pe.wait_ge(consts, 1)
            for n in range(N_FIRST):
                att_unit(n)
                if n == 4:
                    v_to_tokens(3)
                if n >= 4:
                    index_scores(4 * (n - 4))
            v_to_tokens(8)
            v_to_tokens(9)
            for u in range(-1, 16):
                for half in range(2):
                    n = N_FIRST + 2 * u + half
                    if half == 0 and u >= 1:
                        outputs(u - 1)
                    if u + 1 < 16:
                        scores(u + 1, half)
                    if u >= 0:
                        weights(u, half)
                        if n - 1 in V_UNITS and n - 1 >= N_FIRST:
                            v_to_tokens(n - 1)
                        if n < N_ATT:
                            att_unit(n)
            outputs(15)

            late = 0
            for k, (kind, c) in enumerate(MERGE):
                n = N_ATT + k
                if kind == "gate":
                    pe.wait_ge(bank_read, N_ATT + late - 1 if late >= 1 else N_ATT)
                    project(n, late % 2)
                    late += 1
                    continue
                pe.wait_ge(lo_done, n + 1)
                for i, b in enumerate((2, 3, 1, 0)):
                    if c == 0:
                        pe.wait_ge(y_lo_set, 8 if b == 0 else 2 * i + 2)
                    else:
                        pe.wait_ge(merge_step, 4 * c - 3)
                    for c2 in range(2):
                        g = 2 * b + c2
                        cols = slice(g * P, (g + 1) * P)
                        last = three(ps[:, 2 + b, :], w_hi[:, n % RAW, cols], w_lo[:, n % RAW, cols],
                                     y_hi[:, g, :], y_lo[:, g, :], c2 == 0, c2 == 1)
                    last.then_inc(unit_done if i == 3 else branch_full, 1)

            def all_banks(n, l_hi, l_lo, start, stop, in_loop=0):
                s = n % RAW
                for t in range(NT):
                    tile_ = slice(t * P, (t + 1) * P)
                    h = [(ps[:, 2 * t + a, :], w_hi[:, s, a * S:a * S + S], w_lo[:, s, a * S:a * S + S]) for a in range(2)]
                    for o, wh, wl in h:
                        pe.matmul(o, l_hi[:, tile_], wh, start=start, stop=False)
                        pe.matmul(o, l_hi[:, tile_], wl, start=False, stop=False)
                    for o, wh, wl in h:
                        last = pe.matmul(o, l_lo[:, tile_], wh, start=False, stop=stop)
                last.then_inc(unit_done, 1)

            pe.wait_ge(bank_read, N_ATT + 16)
            pe.wait_ge(m_set, KC)
            for c in range(KC):
                pe.wait_ge(lo_done, U_OUT + c + 1)
                all_banks(U_OUT + c, m_hi[:, c, :], m_lo[:, c, :], c == 0, c == KC - 1)
            for t in range(NT):
                pe.wait_ge(h_set, t + 1)
                if t >= 2:
                    pe.wait_ge(hT_lo, t - 1)
                for c in range(KC):
                    last = pe.transpose(ps[:, 2 * (t % 2) + c // 4, (c % 4) * P:(c % 4 + 1) * P],
                                        x_tok[:, t, c * P:(c + 1) * P], ident[:])
                last.then_inc(hT_full, 1)
            pe.wait_ge(hT_lo, NT)
            for h in range(EH):
                if h >= 2:
                    pe.wait_ge(q_lo_set, h - 1)
                project(U_WQ + h, h % 2)
            pe.wait_ge(sk_lo_set, 1)
            pe.wait_ge(q_lo_set, EH)
            for f in range(16):
                t = f // 4
                if f >= 4:
                    pe.wait_ge(sub_set, f - 3)
                for a in range(2):
                    h = 2 * (f % 4) + a
                    tile_ = slice(t * P, (t + 1) * P)
                    last = three(ps[:, 2 + f % 4, 2 * NK * a:2 * NK * a + 2 * NK], q_hi[:, h, tile_], q_lo[:, h, tile_],
                                 sk_hi[:, h, :], sk_lo[:, h, :], True, True)
                last.then_inc(sub_full, 1)

            def expert_unit(j, in_loop, first=False):
                if not first:
                    pe.wait_ge(bank_read, in_loop + BANK_EXP + j - 1)
                project(U_EXP + j, j % 2, in_loop)

            pe.sem_inc(gate_full, 2)
            for k in range(4):
                expert_unit(k, 0, first=k < 2)
            with pe.Fori(0, ROUTE_UNITS // 4 - 1) as i:
                for k in range(4):
                    expert_unit(4 + k, 4 * i)
            pe.wait_ge(sub_set, 16)
            with pe.Fori(0, NT) as b:
                for k in range(8):
                    expert_unit(ROUTE_UNITS + k, 28 * b)
                pe.wait_ge(pick_set, b + 1)
                for k in range(3):
                    last = pe.transpose(ps[:, 4, k * P:(k + 1) * P], pick[:, k, :], ident[:])
                last.then_inc(pickT_full, 1)
                with pe.Fori(0, 2) as i:
                    for body in range(2):
                        for k in range(4):
                            expert_unit(ROUTE_UNITS + 8 + 4 * body + k, 28 * b + 8 * i)
                            for quad in (2 * k, 2 * k + 1):
                                q = 32 * b + 16 * i + 8 * body + quad
                                s = quad % 2
                                pe.wait_ge(right_set, q + 1)
                                pe.wait_ge(right_lo_set, q + 1)
                                pe.wait_ge(gate_read, q + 1)
                                for t in range(4):
                                    o = ps[:, 2 + s, t * P:(t + 1) * P]
                                    pe.matmul(o, left[:, s, t], right_hi[:, s, t], start=True, stop=False)
                                    last = pe.matmul(o, left[:, s, t], right_lo[:, s, t], start=False, stop=True)
                                last.then_inc(gate_full, 1)
                for k in range(4):
                    expert_unit(ROUTE_UNITS + 24 + k, 28 * b)
            for k in range(4):
                expert_unit(124 + k, 0)

            def value_unit(j, in_loop, start=False, stop=False):
                n = U_VAL + j
                pe.wait_ge(lo_done, in_loop + n + 1)
                pe.wait_ge(gh_lo_set, in_loop + j + 1)
                all_banks(n, gh_hi[:, j % 4, :], gh_lo[:, j % 4, :], start, stop, in_loop)

            pe.wait_ge(bank_read, BANK_EXP + P)
            pe.wait_ge(gate_read, 2 + P)
            for k in range(4):
                value_unit(k, 0, start=k == 0)
            with pe.Fori(0, P // 4 - 2) as i:
                for k in range(4):
                    value_unit(4 + k, 4 * i)
            for k in range(P - 4, P):
                value_unit(k, 0, stop=k == P - 1)


def _unit(w):
    return w.reshape(KC, P, P).transpose(1, 0, 2).reshape(P, DM)


def kernel(x, w_in, w_branch, w_out, attn_sinks, ln1_g, ln1_b, peer_wq, peer_subkeys,
           peer_u, peer_v, ln2_g, ln2_b):
    import numpy as np
    import concourse.bacc as bacc
    from concourse.bass_utils import run_bass_kernel_spmd

    a = {k: np.asarray(v) for k, v in dict(
        x=x, w_in=w_in, w_branch=w_branch, w_out=w_out, sinks=attn_sinks, ln1_g=ln1_g, ln1_b=ln1_b,
        wq=peer_wq, subk=peer_subkeys, u=peer_u, v=peer_v, ln2_g=ln2_g, ln2_b=ln2_b).items()}
    names = ["qa", "ka", "va", "qi", "ki", "wi", "qb", "kb", "vb", "qc", "kc", "vc", "qd", "kd", "vd", "g"]
    widths = [256, 64, 64, 256, 32, 8, 256, 128, 128, 256, 256, 256, 256, 256, 256, 4 * DM]
    ends = np.cumsum(widths)
    w = {n: a["w_in"][0][:, e - m:e] for n, m, e in zip(names, widths, ends)}

    def two(n):
        return [w[n][:, :P], w[n][:, P:]]

    cat = lambda *p: np.concatenate(p, axis=1)
    gate = [w["g"][:, (g % 4) * DM + (g // 4) * P:(g % 4) * DM + (g // 4) * P + P] for g in range(32)]
    proj = two("qi") + [cat(w["ki"], w["ki"], w["ki"], w["ki"]), cat(w["va"], w["wi"], w["va"][:, :56])] + \
        two("qc") + two("kc") + two("vc") + two("qd") + two("kd") + two("vd") + two("qb") + \
        [cat(k, k) for k in (w["kb"][:, :64], w["kb"][:, 64:])] + [w["vb"]] + two("qa") + [cat(w["ka"], w["ka"])]
    proj, units = iter(proj), []
    for kind, k in UNITS:
        units.append(_unit(next(proj) if kind == "proj" else gate[k]))
    for kind, c in MERGE:
        if kind == "gate":
            units.append(_unit(gate[c]))
        else:
            b = a["w_branch"][0][:, :, c * P:(c + 1) * P].reshape(8, P, P)
            units.append(b.transpose(1, 0, 2).reshape(P, DM))
    units += list(a["w_out"][0].reshape(KC, P, DM))
    units += [_unit(a["wq"][0][:, h * P:(h + 1) * P]) for h in range(EH)]
    rows = a["x"].reshape(S, DM)
    arrays = {
        "xT": rows.T.reshape(KC, P, S).transpose(1, 0, 2),
        "x_rows": rows,
        "w_units": np.stack(units),
        "u_units": a["u"][0].reshape(P, P, KC, P).transpose(1, 3, 2, 0).reshape(P, P, DM),
        "v_rows": a["v"][0].reshape(P, P, DM),
        "sinks": a["sinks"].reshape(1, NH),
        "ln1_g": a["ln1_g"].reshape(1, DM), "ln1_b": a["ln1_b"].reshape(1, DM),
        "subk": a["subk"][0].transpose(1, 3, 0, 2),
        "ln2_g": a["ln2_g"].reshape(1, DM), "ln2_b": a["ln2_b"].reshape(1, DM),
    }
    arrays = {k: np.ascontiguousarray(v) for k, v in arrays.items()}
    nc = bacc.Bacc("TRN2", target_bir_lowering=False, num_devices=1)
    args = [nc.dram_tensor(k, v.shape, F32, kind="ExternalInput").ap() for k, v in arrays.items()]
    args.append(nc.dram_tensor("gelu_d", (P, P, S), F32, kind="Internal").ap())
    args.append(nc.dram_tensor("gate_d", (NB, P, P, TOK), F32, kind="Internal").ap())
    args.append(nc.dram_tensor("out", (S, DM), F32, kind="ExternalOutput").ap())
    peer_block(nc, *args)
    r = run_bass_kernel_spmd(nc, [arrays], core_ids=[0])
    return r.results[0]["out"].reshape(1, S, DM)
```

```python
import concourse.bass as bass
from concourse import mybir

F32 = mybir.dt.float32
F32R = mybir.dt.float32r
U32 = mybir.dt.uint32
ALU = mybir.AluOpType
ACT = mybir.ActivationFunctionType

P = 128
S = 512
NT = S // P
DM = 1024
KC = DM // P
HD = 64
SCALE = HD ** -0.5
NH = 4
IH, ID = 8, 32
IDX_SCALE = (IH * ID) ** -0.5
TOPK = 128
EH, EK = 8, 16
NK = 128
ALPHA = 2.0 ** 0.25
EPS = 1e-5
BIG = 1.0e30
UNSEEN = -2.0e38
TAKEN = -3.0e38
SLOPES = [2.0 ** (-8.0 * i / 12) for i in range(1, 13)]

N_IDX = 3
N_FIRST = N_IDX + 6
N_FILL = 29
N_ATT = N_FIRST + N_FILL
N_MERGE = 24
U_OUT = N_ATT + N_MERGE
U_WQ = U_OUT + KC
U_EXP = U_WQ + KC
U_VAL = U_EXP + P
U_END = U_VAL + P
RAW = 4
HI_AHEAD = 3
LO_AHEAD = 2
TOK = 32
NB = S // TOK
ROUTE_UNITS = 12
BANK_EXP = N_ATT + 16

HEADS = [("C", h) for h in range(NH)] + [("D", h) for h in range(NH)] + \
        [("B", h) for h in range(NH)] + [("A", h) for h in range(NH)]
Y_SLOT = {"A": 0, "B": 2, "C": 4, "D": 6}
SET = {"C": 0, "B": 0, "D": 6, "A": 6}
SLOPE = {"A": SLOPES[0::3], "B": SLOPES[1::3], "C": SLOPES[2::3]}
V_CHUNK = {"A": 0, "C": 1, "D": 3, "B": 5}

UNITS = [("proj", s) for s in (6, 7, 9)] + [("proj", s) for s in range(6)] + \
        [("proj", 6 + s) for s in range(6)] + [("gate", g) for g in (0, 1)] + \
        [("proj", s) for s in (0, 1, 2, 4)] + [("gate", g) for g in (2, 3, 4)] + \
        [("proj", s) for s in (6, 7, 8)] + [("gate", g) for g in range(5, 16)]
assert len(UNITS) == N_ATT
V_UNITS = {2: (9, 0), 7: (4, 1), 8: (5, 2), 13: (10, 3), 14: (11, 4), 20: (4, 5)}
QK_DONE = {"C": 7, "D": 13, "B": 20, "A": 27}
MERGE = []
for _c in range(KC):
    if _c >= NH:
        MERGE += [("gate", 4 * _c + _n) for _n in range(4)]
    MERGE.append(("branch", _c))
assert len(MERGE) == N_MERGE


Y_SPLIT = {(12, 1): (0, 1), (13, 0): (2,), (13, 1): (3,), (14, 0): (4,), (14, 1): (5,), (15, 0): (6,)}


def keys_of(kind, t):
    return (max(t - 1, 0) * P, (1 if t == 0 else 2) * P) if kind == "B" else (0, (t + 1) * P)


def row_at(kind, t):
    return 2 * P * t if kind == "B" else P * t * (t + 1) // 2


def col_at(kt):
    return S * kt - P * kt * (kt - 1) // 2


def transpose_plan():
    order = [("v", 2), ("v", 7), ("v", 8)]
    for u in range(16):
        order += [("u", u, 0), ("u", u, 1)]
        if N_FIRST + 2 * u - 1 in V_UNITS and u > 0:
            order.append(("v", N_FIRST + 2 * u - 1))
        order += [("u", u, 2), ("u", u, 3)]
        if N_FIRST + 2 * u in V_UNITS:
            order.append(("v", N_FIRST + 2 * u))
    read = {"act": 0, "dve": 0}
    plan = {}
    for i, what in enumerate(order):
        by = "dve" if what[0] == "u" and HEADS[what[1]][0] == "D" else "act"
        read[by] += 1
        plan[what] = (i, by, read[by])
        plan[i] = (by, read[by])
    return plan


def peer_block(nc, xT, x_rows, w_units, u_units, v_rows, sinks, ln1_g, ln1_b, subk, ln2_g, ln2_b,
               gelu_d, gate_d, out):
    plan = transpose_plan()
    base = 16512

    def at(name, kb, shape, dt=F32):
        return nc.alloc_sbuf_tensor_at(name, shape, dt, offset=base + int(kb * 1024))

    raw = at("raw", 0, [P, RAW, DM])
    w_hi = at("w_hi", 16, [P, RAW, DM], F32R)
    w_lo = at("w_lo", 32, [P, RAW, DM], F32R)
    tok_hi = at("tok_hi", 48, [P, KC, S], F32R)
    tok_lo = at("tok_lo", 64, [P, KC, S], F32R)
    R = 80
    projT = at("projT", R + 0, [P, 12, S])
    v_tok = at("v_tok", R + 24, [P, 6, NT, P])
    gates = at("gates", R + 36, [P, 16, S])
    y = at("y", R + 68, [P, 8, S])
    x_raw = at("x_raw", R + 68, [P, KC, S])
    row = [at(f"row{i}", R + 84 + 5 * i, [P, 1280]) for i in range(4)]
    colw = at("colw", R + 104, [P, 1280])
    tmp = at("tmp", R + 109, [P, 2, S])
    dist = at("dist", R + 113, [P, S])
    dist_w = at("dist_w", R + 115, [P, 2 * P])
    dist_a = at("dist_a", R + 116, [P, 1280])
    ident = at("ident", R + 121, [P, P])
    neg_after = at("neg_after", R + 121.5, [P, P])
    neg_ones = at("neg_ones", R + 122, [P, P])
    seen = at("seen", R + 122.5, [P, P])
    hide = at("hide", R + 123, [P, P])
    unseen = at("unseen", R + 123.5, [P, P])
    iota = at("iota", R + 124, [P, P])
    small = at("small", R + 124.5, [P, 160])
    mx, nbias, rsum, esink, rinv = (small[:, 8 * i:8 * i + 8].rearrange("p (a t) -> p a t", a=2) for i in range(5))
    top8 = small[:, 40:48]
    sink_t = small[:, 48:52]
    sink8 = small[:, 52:56]
    stats = small[:, 56:104].rearrange("p (t a s) -> p t a s", t=4, a=2)
    mean_var = small[:, 104:112].rearrange("p (t s) -> p t s", t=4)
    var_eps = small[:, 112:116]
    stdev = small[:, 116:120]
    rstd = small[:, 120:124]
    newton = small[:, 124:128]
    y_hi = [at(f"y_hi{g}", R + kb, [P, S], F32R) for g, kb in enumerate((32, 34, 0, 2, 4, 6, 8, 10))]
    y_lo = [at(f"y_lo{g}", R + kb, [P, S], F32R) for g, kb in enumerate((12, 14, 18, 20, 22, 26, 28, 30))]
    x_tok = at("x_tok", R + 68, [P, NT, DM])
    m_hi = at("m_hi", R + 84, [P, KC, S], F32R)
    m_lo = at("m_lo", R + 100, [P, KC, S], F32R)
    prod = [at("prod0", R + 24, [P, S]), at("prod1", R + 16, [P, S]),
            at("prod2", R + 116, [P, S]), at("prod3", R + 118, [P, S])]
    ln_g = at("ln_g", R + 0, [P, DM])
    ln_b = at("ln_b", R + 4, [P, DM])
    sk_raw = at("sk_raw", R + 8, [P, EH, 2 * NK])
    sk_hi = at("sk_hi", R + 16, [P, EH, 2 * NK], F32R)
    sk_lo = at("sk_lo", R + 24, [P, EH, 2 * NK], F32R)
    q_hi = at("q_hi", R + 84, [P, EH, S], F32R)
    q_lo = at("q_lo", R + 100, [P, EH, S], F32R)
    sub = at("sub", R + 36, [P, NT, 2 * EH * NK])
    left = at("left", R + 0, [P, 2, 4, P], F32R)
    match = at("match", R + 4, [P, 2, 4, P])
    right = at("right", R + 8, [P, 2, 4, 2, P], F32R)
    cand = at("cand", R + 16, [P, EH, EK, EK])
    s_top = at("s_top", R + 24, [P, EH, 2, EK])
    i_top = at("i_top", R + 25, [P, EH, 2, EK], U32)
    c_top = at("c_top", R + 26, [P, EH, EK])
    c_pos = at("c_pos", R + 26.5, [P, EH, EK], U32)
    c_row = at("c_row", R + 27, [P, EH * EK], U32)
    c_col = at("c_col", R + 27.5, [P, EH * EK], U32)
    pick = at("pick", R + 28, [P, 3, P])
    i_T = at("i_T", R + 29.5, [P, 2, P])
    g_hi = at("g_hi", R + 30.5, [P, P], F32R)
    g_lo = at("g_lo", R + 31, [P, P], F32R)
    g_sum = at("g_sum", R + 31.5, [P, 2, EH])
    gelu_t = at("gelu_t", R + 32, [P, 2, S])
    stage = [at(f"stage{i}", R + 84 + 16 * i, [P, P, TOK]) for i in range(2)]
    gate_in = [at(f"gate_in{i}", R + 0 + 8 * i, [P, NB, 4, TOK]) for i in range(2)]
    gelu_in = [at(f"gelu_in{i}", R + 16 + 8 * i, [P, 4, S]) for i in range(2)]
    gh = at("gh", R + 60, [P, 2, S])
    gh_hi = at("gh_hi", R + 36, [P, 4, S], F32R)
    gh_lo = at("gh_lo", R + 44, [P, 4, S], F32R)
    ln2_gt = at("ln2_gt", R + 52, [P, DM])
    ln2_bt = at("ln2_bt", R + 56, [P, DM])
    ps = nc.alloc_psum_tensor("ps", [P, 8, S], F32)

    def sem(name):
        return nc.alloc_semaphore(name)

    const_in, kidx_in, xtok_in, ln_in, sk_in, ln2_in, out_done = (sem(n) for n in (
        "const_in", "kidx_in", "xtok_in", "ln_in", "sk_in", "ln2_in", "out_done"))
    x_in = [sem(f"x_in{i}") for i in range(4)]
    raw_in = [sem(f"raw_in{i}") for i in range(RAW)]
    hi_done, lo_done, unit_done, bank_read = (sem(n) for n in ("hi_done", "lo_done", "unit_done", "bank_read"))
    x_hi, x_lo, consts, const_step, dve_step = (sem(n) for n in (
        "x_hi", "x_lo", "consts", "const_step", "dve_step"))
    score_full, relu_done, idx_added, score_read = (sem(n) for n in (
        "score_full", "relu_done", "idx_added", "score_read"))
    nbias_set, exp_done, sink_exp, probs_set = (sem(n) for n in ("nbias_set", "exp_done", "sink_exp", "probs_set"))
    abs_set, stick_exp, stick_ln, softplus_set, weight_exp = (sem(n) for n in (
        "abs_set", "stick_exp", "stick_ln", "softplus_set", "weight_exp"))
    tp_full, tp_read_act, tp_read_dve, pv_done, y_set = (sem(n) for n in (
        "tp_full", "tp_read_act", "tp_read_dve", "pv_done", "y_set"))
    y_hi_set, y_lo_set, sig_kept, branch_full, merge_step, m_set = (sem(n) for n in (
        "y_hi_set", "y_lo_set", "sig_kept", "branch_full", "merge_step", "m_set"))
    mix_full, norm1_set, scaled1_set = (sem(n) for n in ("mix_full", "norm1_set", "scaled1_set"))
    ffn_full, norm2_set, scaled2_set, last_set = (sem(n) for n in ("ffn_full", "norm2_set", "scaled2_set", "last_set"))
    var_set, std_set, h_set, hT_full, hT_hi, hT_lo = (sem(n) for n in (
        "var_set", "std_set", "h_set", "hT_full", "hT_hi", "hT_lo"))
    sk_zero, sk_hi_set, sk_lo_set, q_hi_set, q_lo_set, sub_full, sub_set = (sem(n) for n in (
        "sk_zero", "sk_hi_set", "sk_lo_set", "q_hi_set", "q_lo_set", "sub_full", "sub_set"))
    gelu_out = [sem(f"gelu_out{i}") for i in range(2)]
    route_step, gexp_in, gexp_done, pick_set, pickT_full, pickT_set = (sem(n) for n in (
        "route_step", "gexp_in", "gexp_done", "pick_set", "pickT_full", "pickT_set"))
    gsum_step, route_seen = sem("gsum_step"), sem("route_seen")
    left_set, match_set, right_set, right_lo_set, gate_full, high_out, gate_read = (sem(n) for n in (
        "left_set", "match_set", "right_set", "right_lo_set", "gate_full", "high_out", "gate_read"))
    stage_out = [sem(f"stage_out{i}") for i in range(2)]
    gate_back = [sem(f"gate_back{i}") for i in range(2)]
    gelu_back = [sem(f"gelu_back{i}") for i in range(2)]
    gh_set, gh_hi_set, gh_lo_set, var2_set, std2_set, out_set = (sem(n) for n in (
        "gh_set", "gh_hi_set", "gh_lo_set", "var2_set", "std2_set", "out_set"))

    def pair_slot(p):
        return Y_SLOT[HEADS[2 * p][0]] + p % 2

    def branch_bank(c, n):
        return ps[:, (2 + n if c >= NH else (7, 6, 4, 5)[n] if c % 2 else (2, 3, 0, 1)[n]), :]

    def score_bank(s):
        return ps[:, 2 + s % 2, :]

    def gate_part(quad, part):
        s = 2 + 2 * (quad % 2)
        return ps[:, s:s + 2, :].rearrange("p c (t a j) -> p (c t) a j", t=2, a=2)[:, :, part, :]

    def softmax_index(u):
        return u if u < 4 else u - 4

    def keys_scored(u, i):
        return 3 - i if HEADS[u][0] == "D" else i

    with nc.Block() as block:

        @block.sync
        def _(sp):
            def load_unit(n, src, in_loop=0):
                if n >= RAW:
                    sp.wait_ge(lo_done, in_loop + n - RAW + 1)
                sp.dma_start(raw[:, n % RAW, :], src).then_inc(raw_in[n % RAW], 16)

            load_unit(0, w_units[0])
            for i in range(4):
                sp.dma_start(x_raw[:, 2 * i:2 * i + 2, :], xT[:, 2 * i:2 * i + 2, :]).then_inc(x_in[i], 16)
            for n in range(1, RAW):
                load_unit(n, w_units[n])
            sp.dma_start(sink_t, sinks.to_broadcast([P, NH])).then_inc(const_in, 16)
            for n in range(RAW, U_OUT):
                load_unit(n, w_units[n])
                if n == U_OUT - 6:
                    sp.wait_ge(y_lo_set, 8)
                    sp.dma_start(x_tok[:], x_rows.rearrange("(t p) d -> p t d", p=P)).then_inc(xtok_in, 16)
            for n in range(U_OUT, U_OUT + 4):
                load_unit(n, w_units[n])
            sp.wait_ge(unit_done, U_OUT)
            sp.dma_start(ln_g[:], ln1_g.to_broadcast([P, DM])).then_inc(ln_in, 16)
            sp.dma_start(ln_b[:], ln1_b.to_broadcast([P, DM])).then_inc(ln_in, 16)
            sp.wait_ge(sk_zero, 1)
            for half in range(2):
                sp.dma_start(sk_raw[HD * half:HD * half + HD, :, NK * half:NK * half + NK],
                             subk[half]).then_inc(sk_in, 16)
            for n in range(U_OUT + 4, U_EXP):
                load_unit(n, w_units[n])
            with sp.Fori(0, P // RAW) as i:
                for k in range(RAW):
                    load_unit(U_EXP + k, u_units[bass.ds(RAW * i + k, 1)].rearrange("a p n -> p (a n)"), RAW * i)

            def load_gates(m, slot, read):
                if read is not None:
                    sp.wait_ge(gh_set, read)
                for s in range(2):
                    sp.wait_ge(gelu_out[s], 32 * m + 32)
                sp.dma_start(gate_in[slot][:], gate_d[:, :, bass.ds(4 * m, 4), :].rearrange("b p j t -> p b j t"))\
                    .then_inc(gate_back[slot], 16)
                sp.dma_start(gelu_in[slot][:], gelu_d[bass.ds(4 * m, 4)].rearrange("j p t -> p j t"))\
                    .then_inc(gelu_back[slot], 16)

            def load_values(m):
                for k in range(RAW):
                    load_unit(U_VAL + k, v_rows[:, bass.ds(4 * m + k, 1), :].rearrange("p a d -> p (a d)"), 4 * m)

            sp.wait_ge(gate_read, 2 + P)
            for s in range(2):
                sp.wait_ge(stage_out[s], 16 * (NB // 2 + 1))
            load_gates(0, 0, None)
            load_values(0)
            load_gates(1, 1, None)
            load_values(1)
            sp.dma_start(ln2_gt[:], ln2_g.to_broadcast([P, DM])).then_inc(ln2_in, 16)
            sp.dma_start(ln2_bt[:], ln2_b.to_broadcast([P, DM])).then_inc(ln2_in, 16)
            with sp.Fori(1, P // 8) as i:
                for half in range(2):
                    m = 2 * i + half
                    load_gates(m, half, 4 * m - 4)
                    load_values(m)
            for t in range(NT):
                if t < NT - 1:
                    sp.wait_ge(out_set, t + 1)
                else:
                    sp.wait_ge(last_set, 1)
                sp.dma_start(out[t * P:(t + 1) * P, :], x_tok[:, t, :]).then_inc(out_done, 16)
            sp.wait_ge(out_done, 16 * NT)

        @block.gpsimd
        def _(pool):
            step = [0]

            def link(ins):
                step[0] += 1
                ins.then_inc(const_step, 1)
                pool.wait_ge(const_step, step[0])

            def select(t, op, fill, base, pattern, mult):
                link(pool.affine_select(out=t, in_=t, compare_op=op, fill=fill, base=base, pattern=pattern,
                                        channel_multiplier=mult))

            def split_lo(n, in_loop=0):
                pool.wait_ge(hi_done, in_loop + n + 1)
                pool.tensor_tensor(w_lo[:, n % RAW, :], raw[:, n % RAW, :], w_hi[:, n % RAW, :].bitcast(F32),
                                   ALU.subtract).then_inc(lo_done, 1)

            def times_g(t, g_tile, norm_sem, done):
                pool.wait_ge(norm_sem, t + 1)
                pool.tensor_tensor(x_tok[:, t, :], x_tok[:, t, :], g_tile[:], ALU.mult).then_inc(done, 1)

            exact = dict(allow_small_or_imprecise_dtypes=True)
            link(pool.memset(ident[:], 0.0))
            select(ident[:], ALU.not_equal, 1.0, 0, [[-1, P]], 1)
            split_lo(0)
            link(pool.iota(dist[:], pattern=[[-1, S]], base=S - P, channel_multiplier=1, **exact))
            select(dist[:], ALU.is_ge, BIG, S - P, [[-1, S]], 1)
            link(pool.memset(unseen[:], 0.0))
            select(unseen[:], ALU.is_ge, UNSEEN, 0, [[-1, P]], 1)
            split_lo(1)
            link(pool.iota(dist_w[:], pattern=[[-1, 2 * P]], base=P, channel_multiplier=1, **exact))
            select(dist_w[:], ALU.is_ge, BIG, P, [[-1, 2 * P]], 1)
            select(dist_w[:], ALU.is_gt, BIG, 0, [[1, 2 * P]], -1)
            split_lo(2)
            link(pool.memset(seen[:], 1.0))
            select(seen[:], ALU.is_gt, 0.0, 0, [[1, P]], -1)
            link(pool.memset(hide[:], 0.0))
            select(hide[:], ALU.is_gt, -BIG, 0, [[1, P]], -1)
            split_lo(3)
            link(pool.memset(neg_after[:], -1.0))
            select(neg_after[:], ALU.is_gt, 0.0, 0, [[-1, P]], 1)
            link(pool.memset(neg_ones[:], -1.0))
            pool.iota(iota[:], pattern=[[1, P]], base=0, channel_multiplier=0, **exact).then_inc(consts, 1)
            for n in range(4, U_EXP + LO_AHEAD):
                if n in (U_WQ, U_WQ + 1):
                    for t in ((0, 1) if n == U_WQ else (2,)):
                        times_g(t, ln_g, norm1_set, scaled1_set)
                if n == U_WQ + 5:
                    pool.wait_ge(sk_hi_set, 1)
                    pool.tensor_tensor(sk_lo[:], sk_raw[:], sk_hi[:].bitcast(F32), ALU.subtract)\
                        .then_inc(sk_lo_set, 1)
                if n == U_OUT + 4:
                    pool.wait_ge(unit_done, U_OUT)
                    pool.memset(sk_raw[:], 0.0).then_inc(sk_zero, 1)
                split_lo(n)

            def plain(count, first, in_loop):
                for k in range(count):
                    split_lo(first + k + LO_AHEAD, in_loop)

            with pool.Fori(0, ROUTE_UNITS // 4) as i:
                plain(4, U_EXP, 4 * i)
            with pool.Fori(0, NT) as b:
                plain(8, U_EXP + ROUTE_UNITS, 28 * b)
                with pool.Fori(0, 2) as i:
                    for body in range(2):
                        for k in range(4):
                            split_lo(U_EXP + ROUTE_UNITS + 8 + 4 * body + k + LO_AHEAD, 28 * b + 8 * i)
                            for quad in (2 * k, 2 * k + 1):
                                q = 32 * b + 16 * i + 8 * body + quad
                                pool.wait_ge(match_set, q + 1)
                                pool.tensor_tensor(
                                    right[:, quad % 2, :, 0, :], match[:, quad % 2],
                                    g_hi[:, bass.ds(64 * i + 32 * body + 4 * quad, 4)].bitcast(F32)
                                    .unsqueeze(2).to_broadcast([P, 4, P]), ALU.mult).then_inc(right_set, 1)
                plain(4, U_EXP + ROUTE_UNITS + 24, 28 * b)
            plain(4, U_EXP + 124, 0)
            with pool.Fori(0, (P - 4) // 4) as i:
                plain(4, U_VAL, 4 * i)
            for k in range(4 - LO_AHEAD):
                split_lo(U_END - 4 + LO_AHEAD + k)
            for t in range(NT - 1):
                times_g(t, ln2_gt, norm2_set, scaled2_set)
                pool.wait_ge(scaled2_set, t + 1)
                pool.tensor_tensor(x_tok[:, t, :], x_tok[:, t, :], ln2_bt[:], ALU.add).then_inc(out_set, 1)

        @block.scalar
        def _(act):
            def split_hi(n, in_loop=0):
                act.wait_ge(raw_in[n % RAW], 4 * in_loop + 16 * (n // RAW + 1))
                if n >= RAW:
                    act.wait_ge(unit_done, in_loop + n - RAW + 1)
                act.activation(w_hi[:, n % RAW, :], raw[:, n % RAW, :], ACT.Copy).then_inc(hi_done, 1)

            def projected(n):
                kind, k = UNITS[n]
                act.wait_ge(unit_done, n + 1)
                act.activation(projT[:, k, :] if kind == "proj" else gates[:, k, :], ps[:, n % 2, :], ACT.Copy)\
                    .then_inc(bank_read, 1)

            def v_to_tokens(n):
                i = plan["v", n][0]
                act.wait_ge(tp_full, i + 1)
                act.activation(v_tok[:, V_UNITS[n][1]], ps[:, 4 + i % 2, :].rearrange("p (t c) -> p t c", t=NT),
                               ACT.Copy).then_inc(tp_read_act, 1)

            def relu_scores(first):
                for s in range(first, first + 4):
                    act.wait_ge(score_full, s + 1)
                    if s >= 2:
                        act.wait_ge(idx_added, s - 1)
                    n = (s // IH + 2) * P
                    act.activation(tmp[:, s % 2, :n], score_bank(s)[:, :n], ACT.Relu, scale=IDX_SCALE)\
                        .then_inc(relu_done, 1)

            def exponents(u, half):
                kind, h = HEADS[u]
                if kind != "D":
                    su = softmax_index(u)
                    act.wait_ge(nbias_set, 2 * su + half + 1)
                    for t in (2 * half, 2 * half + 1):
                        n, o = keys_of(kind, t)[1], row_at(kind, t)
                        act.activation(row[u % 2][:, o:o + n], row[u % 2][:, o:o + n], ACT.Exp, scale=SCALE,
                                       bias=nbias[:, u % 2, t:t + 1], accum_out=rsum[:, u % 2, t:t + 1])\
                            .then_inc(exp_done, 1)
                        if kind == "B":
                            act.activation(esink[:, u % 2, t:t + 1], sink_t[:, h:h + 1], ACT.Exp,
                                           bias=nbias[:, u % 2, t:t + 1]).then_inc(sink_exp, 1)
                else:
                    d = 4 * (u - 4) + 2 * half
                    for i in range(2):
                        kt = keys_scored(u, 2 * half + i)
                        o, n = col_at(kt), S - kt * P
                        act.wait_ge(abs_set, d + i + 1)
                        act.activation(row[2 + u % 2][:, o:o + n], row[2 + u % 2][:, o:o + n], ACT.Exp)\
                            .then_inc(stick_exp, 1)
                    for i in range(2):
                        kt = keys_scored(u, 2 * half + i)
                        o, n = col_at(kt), S - kt * P
                        act.wait_ge(stick_exp, d + i + 1)
                        act.activation(row[2 + u % 2][:, o:o + n], row[2 + u % 2][:, o:o + n], ACT.Ln, bias=1.0)\
                            .then_inc(stick_ln, 1)

            def weights(u, half):
                kind, _ = HEADS[u]
                for i in (2 * half, 2 * half + 1):
                    idx, _, reads = plan["u", u, i]
                    if kind != "D":
                        n = (S - i * P) if kind != "B" else min(2, NT - i) * P
                        act.wait_ge(tp_full, idx + 1)
                        act.activation(colw[:, col_at(i):col_at(i) + n], ps[:, 4 + idx % 2, i * P:i * P + n],
                                       ACT.Copy).then_inc(tp_read_act, 1)
                    else:
                        kt = keys_scored(u, i)
                        o, n = col_at(kt), S - kt * P
                        act.wait_ge(tp_read_dve, reads)
                        act.activation(colw[:, o:o + n], colw[:, o:o + n], ACT.Exp).then_inc(weight_exp, 1)

            def unit(n):
                if n + HI_AHEAD < U_END:
                    split_hi(n + HI_AHEAD)
                projected(n)

            act.preload_act_table_set("natural_log_exp_and_others")
            split_hi(0)
            for c in range(0, KC, 2):
                act.wait_ge(x_in[c // 2], 16)
                act.activation(tok_hi[:, c:c + 2, :], x_raw[:, c:c + 2, :], ACT.Copy).then_inc(x_hi, 1)
            for n in range(1, HI_AHEAD):
                split_hi(n)
            act.wait_ge(const_in, 16)
            for n in range(N_FIRST):
                unit(n)
                if n == N_IDX - 1:
                    act.wait_ge(bank_read, N_IDX)
                    for r in range(0, P, ID):
                        act.dma_start(projT[r:r + ID, 8, :], projT[HD:HD + ID, 9, :]).then_inc(kidx_in, 16)
                if n == N_IDX:
                    v_to_tokens(2)
                if n >= N_IDX:
                    relu_scores(4 * (n - N_IDX))
            v_to_tokens(7)
            v_to_tokens(8)
            for u in range(-1, 16):
                for half in range(2):
                    n = N_FIRST + 2 * u + half
                    if u + 1 < 16:
                        exponents(u + 1, half)
                    if u >= 0:
                        weights(u, half)
                        if n < N_ATT:
                            unit(n)
                        if n - 1 in V_UNITS and n - 1 >= N_FIRST:
                            v_to_tokens(n - 1)
                        if u == 15 and half == 0:
                            split_hi(N_ATT + HI_AHEAD)
                    for p in Y_SPLIT.get((u, half), ()):
                        act.wait_ge(y_set, p + 1)
                        act.activation(y_hi[pair_slot(p)][:], y[:, pair_slot(p), :], ACT.Copy).then_inc(y_hi_set, 1)

            act.activation(gates[:, 0:4, :], gates[:, 0:4, :], ACT.Sigmoid).then_inc(sig_kept, 1)
            act.wait_ge(pv_done, 16)
            act.activation(y_hi[pair_slot(7)][:], ps[:, 7, :], ACT.Copy).then_inc(y_hi_set, 1)
            late = 0
            for k, (kind, c) in enumerate(MERGE):
                n = N_ATT + k
                if k > 0:
                    split_hi(n + HI_AHEAD)
                if kind == "gate":
                    act.wait_ge(unit_done, n + 1)
                    act.wait_ge(merge_step, 4 * (c // 4 - NH) + 1)
                    act.activation(gates[:, c - 16, :], ps[:, late % 2, :], ACT.Sigmoid).then_inc(bank_read, 1)
                    late += 1
                elif c + 1 < NH:
                    act.activation(gates[:, 4 * c + 4:4 * c + 8, :], gates[:, 4 * c + 4:4 * c + 8, :], ACT.Sigmoid)\
                        .then_inc(sig_kept, 1)
            for n in range(U_OUT, U_WQ - HI_AHEAD):
                split_hi(n + HI_AHEAD)
            act.wait_ge(sk_in, 32)
            act.wait_ge(m_set, KC)
            act.activation(sk_hi[:], sk_raw[:], ACT.Copy).then_inc(sk_hi_set, 1)

            def root(t, var_sem, std_sem):
                act.wait_ge(var_sem, t + 1)
                act.activation(stdev[:, t:t + 1], var_eps[:, t:t + 1], ACT.Sqrt).then_inc(std_sem, 1)

            def hT_high(t):
                act.wait_ge(hT_full, t + 1)
                act.activation(tok_hi[:, :, t * P:(t + 1) * P],
                               ps[:, 2 * t:2 * t + 2, :].rearrange("p a (c q) -> p (a c) q", c=4), ACT.Copy)\
                    .then_inc(hT_hi, 1)

            root(0, var_set, std_set)
            root(1, var_set, std_set)
            hT_high(0)
            root(2, var_set, std_set)
            split_hi(U_WQ)
            split_hi(U_WQ + 1)
            hT_high(1)
            split_hi(U_WQ + 2)
            split_hi(U_WQ + 3)
            root(3, var_set, std_set)
            hT_high(2)
            hT_high(3)
            for h in range(EH):
                n = U_WQ + h
                if h >= 1:
                    split_hi(n + HI_AHEAD)
                act.wait_ge(unit_done, n + 1)
                act.activation(q_hi[:, h, :], ps[:, h, :], ACT.Copy).then_inc(q_hi_set, 1)
            for f in range(16):
                act.wait_ge(sub_full, f + 1)
                act.activation(sub[:, f // 4, S * (f % 4):S * (f % 4) + S], ps[:, 2 + f % 4, :], ACT.Copy)\
                    .then_inc(sub_set, 1)

            def expert_unit(j, in_loop, first=False, before=lambda: None):
                n = U_EXP + j
                split_hi(n + HI_AHEAD, in_loop)
                before()
                act.wait_ge(unit_done, in_loop + n + 1)
                if not first or j >= 2:
                    act.wait_ge(gelu_out[j % 2], 8 * in_loop + 16 * (j // 2))
                act.activation(gelu_t[:, j % 2, :], ps[:, j % 2, :], ACT.Gelu).then_inc(bank_read, 1)
                act.wait_ge(bank_read, in_loop + BANK_EXP + j + 1)
                act.dma_start(gelu_d[bass.ds(in_loop + j, 1)].rearrange("a p t -> p (a t)"), gelu_t[:, j % 2, :])\
                    .then_inc(gelu_out[j % 2], 16)

            def right_low(b, body, k):
                for quad in (2 * k, 2 * k + 1):
                    act.wait_ge(match_set, 32 * b + 8 * body + quad + 1)
                    for t in range(4):
                        tok = TOK * body + 4 * quad + t
                        last = act.activation(right[:, quad % 2, t, 1, :], match[:, quad % 2, t, :], ACT.Copy,
                                              scale=g_lo[:, tok:tok + 1].bitcast(F32))
                    last.then_inc(right_lo_set, 1)

            def store_gates(b, body):
                act.wait_ge(gate_read, 32 * b + 8 * body + 8 + 2)
                act.dma_start(gate_d[bass.ds(4 * b + body, 1)].rearrange("a p j t -> p (a j t)"),
                              stage[body % 2][:].rearrange("p j t -> p (j t)")).then_inc(stage_out[body % 2], 16)

            for s in range(2):
                act.sem_inc(stage_out[s], 16)
            for k in range(4):
                expert_unit(k, 0, first=True)
            with act.Fori(0, ROUTE_UNITS // 4 - 1) as i:
                for k in range(4):
                    expert_unit(4 + k, 4 * i)
            with act.Fori(0, NT) as b:
                for k in range(4):
                    expert_unit(ROUTE_UNITS + k, 28 * b)
                act.wait_ge(gexp_in, b + 1)
                act.activation(pick[:, 2, :], pick[:, 2, :], ACT.Exp).then_inc(gexp_done, 1)
                for k in range(4, 8):
                    expert_unit(ROUTE_UNITS + k, 28 * b)
                for body in range(4):
                    for k in range(4):
                        expert_unit(ROUTE_UNITS + 8 + 4 * body + k, 28 * b, before=lambda: right_low(b, body, k))
                        if k == 0:
                            if body >= 1:
                                store_gates(b, body - 1)
                            act.wait_ge(stage_out[body % 2], 32 * b + 16 * (body // 2) + 16)
                        for quad in (2 * k, 2 * k + 1):
                            act.wait_ge(gate_full, 32 * b + 8 * body + quad + 3)
                            act.activation(
                                stage[body % 2][:, :, 4 * quad:4 * quad + 4].rearrange("p j t -> p t j"),
                                gate_part(quad, 0), ACT.Copy).then_inc(high_out, 1)
                expert_unit(ROUTE_UNITS + 24, 28 * b)
                store_gates(b, 3)
                for k in range(1, 4):
                    expert_unit(ROUTE_UNITS + 24 + k, 28 * b)
            for k in range(3):
                expert_unit(124 + k, 0)

            def gh_high(j, in_loop):
                act.wait_ge(gh_set, in_loop + j + 1)
                act.wait_ge(unit_done, in_loop + U_VAL + j - 3)
                act.activation(gh_hi[:, j % 4, :], gh[:, j % 2, :], ACT.Copy).then_inc(gh_hi_set, 1)

            gh_high(0, 0)
            gh_high(1, 0)
            expert_unit(P - 1, 0)
            with act.Fori(0, (P - 4) // 4) as i:
                for k in range(4):
                    split_hi(U_VAL + k + HI_AHEAD, 4 * i)
                    gh_high(k + 2, 4 * i)
            split_hi(U_END - 1)
            for j in (P - 2, P - 1):
                gh_high(j, 0)
            for t in range(NT):
                root(t, var2_set, std2_set)

        @block.vector
        def _(dve):
            step = [0]

            def link(ins):
                step[0] += 1
                ins.then_inc(dve_step, 1)
                dve.wait_ge(dve_step, step[0])

            for c in range(0, KC, 2):
                dve.wait_ge(x_hi, c // 2 + 1)
                dve.tensor_tensor(tok_lo[:, c:c + 2, :], x_raw[:, c:c + 2, :], tok_hi[:, c:c + 2, :].bitcast(F32),
                                  ALU.subtract).then_inc(x_lo, 1)
            dve.wait_ge(const_in, 16)
            link(dve.tensor_scalar(sink8, sink_t, 1.0 / SCALE, None, ALU.mult))
            dve.wait_ge(consts, 1)
            link(dve.tensor_copy(dist_a[:, 0:P], dist[:, S - P:S]))

            dve.wait_ge(tp_read_act, 1)
            for s in range(3 * IH):
                t, h = s // IH + 1, s % IH
                n, o = (t + 1) * P, row_at("A", t)
                w = v_tok[:, 0, t, HD + ID + h:HD + ID + h + 1]
                dve.wait_ge(relu_done, s + 1)
                acc = dist_a[:, o:o + n]
                if h == 0:
                    ins = dve.tensor_scalar(acc, tmp[:, s % 2, :n], w, None, ALU.mult)
                else:
                    ins = dve.scalar_tensor_tensor(acc, tmp[:, s % 2, :n], w, acc, ALU.mult, ALU.add)
                ins.then_inc(idx_added, 1)
                dve.wait_ge(idx_added, s + 1)
                if h == IH - 1:
                    link(dve.tensor_tensor(dist_a[:, o + n - P:o + n], dist_a[:, o + n - P:o + n], unseen[:], ALU.add))

            def choose_keys(r):
                t = r // (TOPK // 8) + 1
                n, o = (t + 1) * P, row_at("A", t)
                left_over = dist_a[:, o:o + n]
                link(dve.max(top8, left_over))
                link(dve.match_replace(left_over, top8, left_over, TAKEN))
                if r % (TOPK // 8) == TOPK // 8 - 1:
                    link(dve.tensor_scalar(left_over, left_over, 0.5 * (TAKEN + UNSEEN), BIG, ALU.is_gt, ALU.mult))
                    link(dve.tensor_tensor(left_over, left_over, dist[:, S - n:S], ALU.add))

            def scores(u, half):
                kind, h = HEADS[u]
                s0 = 24 + 4 * u + 2 * half
                if kind != "D":
                    src = {"A": dist_a[:], "B": dist_w[:], "C": dist[:]}[kind]
                    width = {"A": 1280, "B": 2 * P, "C": S}[kind]
                    bias = row[2][:, :width]
                    if half == 0:
                        link(dve.tensor_scalar(bias, src, -SLOPE[kind][h] / SCALE, None, ALU.mult))
                    for i in range(2):
                        t = 2 * half + i
                        n, o = keys_of(kind, t)[1], row_at(kind, t)
                        b = bias[:, o:o + n] if kind == "A" else bias[:, width - n:width]
                        dve.wait_ge(score_full, s0 + i + 1)
                        dve.tensor_tensor_reduce(
                            out=row[u % 2][:, o:o + n], in0=score_bank(s0 + i)[:, :n], in1=b, scale=1.0,
                            scalar=-3.0e38, op0=ALU.add, op1=ALU.max, accum_out=mx[:, u % 2, t:t + 1])\
                            .then_inc(score_read, 1)
                    dve.wait_ge(score_read, 4 * u + 2 * half + 2)
                    two = slice(2 * half, 2 * half + 2)
                    if kind == "B":
                        ins = dve.tensor_scalar(nbias[:, u % 2, two], mx[:, u % 2, two], sink8[:, h:h + 1], -SCALE,
                                                ALU.max, ALU.mult)
                    else:
                        ins = dve.tensor_scalar(nbias[:, u % 2, two], mx[:, u % 2, two], -SCALE, None, ALU.mult)
                    ins.then_inc(nbias_set, 1)
                else:
                    for i in range(2):
                        kt = keys_scored(u, 2 * half + i)
                        o, n = col_at(kt), S - kt * P
                        dve.wait_ge(score_full, s0 + i + 1)
                        dve.tensor_scalar(tmp[:, i, :n], score_bank(s0 + i)[:, :n], SCALE, None, ALU.mult)\
                            .then_inc(score_read, 1)
                        dve.wait_ge(score_read, 4 * u + 2 * half + i + 1)
                        dve.scalar_tensor_tensor(row[2 + u % 2][:, o:o + n], tmp[:, i, :n], -1.0, tmp[:, i, :n],
                                                 ALU.mult, ALU.min).then_inc(abs_set, 1)

            def scores_end(u, half):
                kind, h = HEADS[u]
                if kind != "D":
                    su = softmax_index(u)
                    two = slice(2 * half, 2 * half + 2)
                    dve.wait_ge(exp_done, 4 * su + 2 * half + 2)
                    if kind == "B":
                        dve.wait_ge(sink_exp, 4 * h + 2 * half + 2)
                        link(dve.tensor_tensor(rsum[:, u % 2, two], rsum[:, u % 2, two], esink[:, u % 2, two], ALU.add))
                    link(dve.reciprocal(rinv[:, u % 2, two], rsum[:, u % 2, two]))
                    for t in (2 * half, 2 * half + 1):
                        n, o = keys_of(kind, t)[1], row_at(kind, t)
                        dve.tensor_scalar(row[u % 2][:, o:o + n], row[u % 2][:, o:o + n], rinv[:, u % 2, t:t + 1],
                                          None, ALU.mult).then_inc(probs_set, 1)
                else:
                    d = 4 * (u - 4) + 2 * half
                    for i in range(2):
                        kt = keys_scored(u, 2 * half + i)
                        o, n = col_at(kt), S - kt * P
                        sp_, ls = row[u % 2], row[2 + u % 2]
                        dve.wait_ge(stick_ln, d + i + 1)
                        link(dve.scalar_tensor_tensor(sp_[:, o:o + n], tmp[:, i, :n], 0.0, ls[:, o:o + n],
                                                      ALU.max, ALU.add))
                        dve.tensor_tensor(sp_[:, o:o + P], sp_[:, o:o + P], seen[:], ALU.mult)\
                            .then_inc(softplus_set, 1)
                        link(dve.scalar_tensor_tensor(ls[:, o:o + n], tmp[:, i, :n], 0.0, ls[:, o:o + n],
                                                      ALU.min, ALU.subtract))
                        link(dve.tensor_tensor(ls[:, o:o + P], ls[:, o:o + P], hide[:], ALU.add))

            def weights(u, half):
                if HEADS[u][0] != "D":
                    return
                for i in (2 * half, 2 * half + 1):
                    kt = keys_scored(u, i)
                    o, n = col_at(kt), S - kt * P
                    idx = plan["u", u, i][0]
                    dve.wait_ge(tp_full, idx + 1)
                    dve.tensor_tensor(colw[:, o:o + n], ps[:, 4 + idx % 2, :n], row[2 + u % 2][:, o:o + n],
                                      ALU.add).then_inc(tp_read_dve, 1)

            def store_y(p):
                dve.wait_ge(pv_done, 2 * p + 2)
                dve.tensor_copy(y[:, pair_slot(p), :], ps[:, 6 + p % 2, :]).then_inc(y_set, 1)

            def y_low(p, y_):
                dve.wait_ge(y_hi_set, p + 1)
                dve.tensor_tensor(y_lo[pair_slot(p)][:], y_, y_hi[pair_slot(p)][:].bitcast(F32), ALU.subtract)\
                    .then_inc(y_lo_set, 1)

            r = 0
            for u in range(-1, 16):
                for half in range(2):
                    if u + 1 < 16:
                        scores(u + 1, half)
                    if u >= 0:
                        weights(u, half)
                    if half == 1 and u >= 2 and u % 2 == 0:
                        store_y(u // 2 - 1)
                    if u >= 0:
                        for _ in range(2 + half):
                            if r < 3 * TOPK // 8:
                                choose_keys(r)
                                r += 1
                    if u + 1 < 16:
                        scores_end(u + 1, half)
                    for p in Y_SPLIT.get((u, half), ()):
                        y_low(p, y[:, pair_slot(p), :])
                assert u < 10 or r == 3 * TOPK // 8

            y_low(7, ps[:, 7, :])
            for c in range(KC):
                for k, n in enumerate((2, 3, 1, 0)):
                    if k < 3:
                        dve.wait_ge(branch_full, 3 * c + k + 1)
                    else:
                        dve.wait_ge(unit_done, N_ATT + MERGE.index(("branch", c)) + 1)
                    if c < NH:
                        dve.wait_ge(sig_kept, c + 1)
                    else:
                        dve.wait_ge(bank_read, N_ATT + 4 * (c - NH) + n + 1)
                    slot = (4 * c + n) % 16
                    dve.tensor_tensor(prod[n][:], branch_bank(c, n), gates[:, slot, :], ALU.mult).then_inc(dve_step, 1)
                    step[0] += 1
                dve.wait_ge(dve_step, step[0])
                dve.tensor_tensor(prod[0][:], prod[0][:], prod[1][:], ALU.add).then_inc(merge_step, 1)
                dve.wait_ge(merge_step, 4 * c + 1)
                dve.tensor_tensor(prod[2][:], prod[2][:], prod[3][:], ALU.add).then_inc(merge_step, 1)
                dve.wait_ge(merge_step, 4 * c + 2)
                dve.tensor_tensor(prod[0][:], prod[0][:], prod[2][:], ALU.add).then_inc(merge_step, 1)
                dve.wait_ge(merge_step, 4 * c + 3)
                dve.tensor_copy(m_hi[:, c, :], prod[0][:]).then_inc(merge_step, 1)
                dve.wait_ge(merge_step, 4 * c + 4)
                dve.tensor_tensor(m_lo[:, c, :], prod[0][:], m_hi[:, c, :].bitcast(F32), ALU.subtract).then_inc(m_set, 1)
                dve.wait_ge(m_set, c + 1)

            def norm(t, full, var_sem, std_sem, done, meanwhile=lambda: None):
                if t < NT - 1:
                    dve.wait_ge(full[0], t + 1)
                else:
                    dve.wait_ge(unit_done, full[1])
                z, one = x_tok[:, t, :], slice(t, t + 1)
                link(dve.scalar_tensor_tensor(
                    z.rearrange("p (a n) -> p a n", a=2), z.rearrange("p (a n) -> p a n", a=2), ALPHA,
                    ps[:, 2 * t:2 * t + 2, :], ALU.mult, ALU.add))
                dve.bn_stats(stats[:, t, 0], x_tok[:, t, 0:S])
                link(dve.bn_stats(stats[:, t, 1], x_tok[:, t, S:DM]))
                link(dve.bn_aggr(mean_var[:, t], stats[:, t]))
                dve.tensor_scalar(var_eps[:, one], mean_var[:, t, 1:2], EPS, None, ALU.add).then_inc(var_sem, 1)
                meanwhile()
                dve.wait_ge(std_sem, t + 1)
                link(dve.reciprocal(rstd[:, one], stdev[:, one]))
                link(dve.scalar_tensor_tensor(newton[:, one], rstd[:, one], var_eps[:, one], rstd[:, one],
                                              ALU.mult, ALU.mult))
                link(dve.tensor_scalar(newton[:, one], newton[:, one], -0.5, 1.5, ALU.mult, ALU.add))
                link(dve.tensor_tensor(rstd[:, one], rstd[:, one], newton[:, one], ALU.mult))
                dve.tensor_scalar(z, z, mean_var[:, t, 0:1], rstd[:, one], ALU.subtract, ALU.mult).then_inc(done, 1)
                if t == NT - 1:
                    dve.wait_ge(done, t + 1)

            def plus_b(t, b_tile, scaled, done):
                dve.wait_ge(scaled, t + 1)
                dve.tensor_tensor(x_tok[:, t, :], x_tok[:, t, :], b_tile[:], ALU.add).then_inc(done, 1)

            def last_tile(g_tile, b_tile, done):
                link(dve.tensor_tensor(x_tok[:, NT - 1, :], x_tok[:, NT - 1, :], g_tile[:], ALU.mult))
                dve.tensor_tensor(x_tok[:, NT - 1, :], x_tok[:, NT - 1, :], b_tile[:], ALU.add).then_inc(done, 1)

            def hT_low(t):
                dve.wait_ge(hT_hi, t + 1)
                dve.tensor_tensor(tok_lo[:, :, t * P:(t + 1) * P],
                                  ps[:, 2 * t:2 * t + 2, :].rearrange("p a (c q) -> p (a c) q", c=4),
                                  tok_hi[:, :, t * P:(t + 1) * P].bitcast(F32), ALU.subtract).then_inc(hT_lo, 1)

            mix = ((mix_full, U_WQ), var_set, std_set, norm1_set)
            dve.wait_ge(xtok_in, 16)
            dve.wait_ge(ln_in, 32)
            norm(0, *mix)
            norm(1, *mix, meanwhile=lambda: plus_b(0, ln_b, scaled1_set, h_set))
            norm(2, *mix, meanwhile=lambda: plus_b(1, ln_b, scaled1_set, h_set))
            hT_low(0)
            hT_low(1)
            norm(3, *mix, meanwhile=lambda: plus_b(2, ln_b, scaled1_set, h_set))
            last_tile(ln_g, ln_b, h_set)
            hT_low(2)
            hT_low(3)
            for h in range(EH):
                dve.wait_ge(q_hi_set, h + 1)
                dve.tensor_tensor(q_lo[:, h, :], ps[:, h, :], q_hi[:, h, :].bitcast(F32), ALU.subtract)\
                    .then_inc(q_lo_set, 1)

            ROUTE_STEPS = 18

            def route(b):
                n_step = [0]

                def settled(ins):
                    n_step[0] += 1
                    ins.then_inc(route_step, 1)
                    dve.wait_ge(route_step, ROUTE_STEPS * b + n_step[0])
                    dve.sem_inc(route_seen, 1)

                halves = [(h, p) for h in range(EH) for p in range(2)]
                work = cand[:].rearrange("p h a c -> p (h a c)").rearrange("p (h s k) -> p h s k", h=EH, s=2)
                settled(dve.tensor_copy(cand[:].rearrange("p h a c -> p (h a c)"),
                                        sub[:, bass.ds(b, 1), :].rearrange("p a n -> p (a n)")))
                for h, p in halves:
                    ins = dve.max(s_top[:, h, p, 0:8], work[:, h, p, :])
                settled(ins)
                for h, p in halves:
                    ins = dve.max_index(i_top[:, h, p, 0:8], s_top[:, h, p, 0:8], work[:, h, p, :])
                settled(ins)
                for h, p in halves:
                    ins = dve.match_replace(work[:, h, p, :], s_top[:, h, p, 0:8], work[:, h, p, :], TAKEN)
                settled(ins)
                for h, p in halves:
                    ins = dve.max(s_top[:, h, p, 8:16], work[:, h, p, :])
                settled(ins)
                for h, p in halves:
                    ins = dve.max_index(i_top[:, h, p, 8:16], s_top[:, h, p, 8:16], work[:, h, p, :])
                settled(ins)
                settled(dve.tensor_tensor(
                    cand[:], s_top[:, :, 0, :].unsqueeze(3).to_broadcast([P, EH, EK, EK]),
                    s_top[:, :, 1, :].unsqueeze(2).to_broadcast([P, EH, EK, EK]), ALU.add))
                rows = cand[:].rearrange("p h a c -> p h (a c)")
                for h in range(EH):
                    ins = dve.max(c_top[:, h, 0:8], rows[:, h, :])
                settled(ins)
                for h in range(EH):
                    ins = dve.max_index(c_pos[:, h, 0:8], c_top[:, h, 0:8], rows[:, h, :])
                settled(ins)
                for h in range(EH):
                    ins = dve.match_replace(rows[:, h, :], c_top[:, h, 0:8], rows[:, h, :], TAKEN)
                settled(ins)
                for h in range(EH):
                    ins = dve.max(c_top[:, h, 8:16], rows[:, h, :])
                settled(ins)
                dve.tensor_tensor(pick[:, 2, :].rearrange("p (h k) -> p h k", h=EH), c_top[:],
                                  c_top[:, :, 0:1].to_broadcast([P, EH, EK]), ALU.subtract).then_inc(gexp_in, 1)
                for h in range(EH):
                    ins = dve.max_index(c_pos[:, h, 8:16], c_top[:, h, 8:16], rows[:, h, :])
                settled(ins)
                pos = c_pos[:].rearrange("p h k -> p (h k)")
                dve.tensor_scalar(c_row[:], pos, 4, None, ALU.logical_shift_right)
                settled(dve.tensor_scalar(c_col[:], pos, EK - 1, None, ALU.bitwise_and))
                for p, rank in ((0, c_row), (1, c_col)):
                    hot = cand[:].rearrange("p h a c -> p (h a) c")
                    settled(dve.tensor_tensor(hot, rank[:].unsqueeze(2).to_broadcast([P, EH * EK, EK]),
                                              iota[:, 0:EK].unsqueeze(1).to_broadcast([P, EH * EK, EK]),
                                              ALU.is_equal))
                    settled(dve.tensor_tensor(cand[:], cand[:],
                                              i_top[:, :, p, :].unsqueeze(2).to_broadcast([P, EH, EK, EK]), ALU.mult))
                    ins = dve.tensor_reduce(pick[:, p, :], hot, mybir.AxisListType.X, ALU.add)
                    if p == 0:
                        settled(ins)
                dve.wait_ge(gexp_done, b + 1)
                g = pick[:, 2, :].rearrange("p (h k) -> p h k", h=EH)
                settled2(dve.tensor_reduce(g_sum[:, 0, :], g, mybir.AxisListType.X, ALU.add), b, 1)
                settled2(dve.reciprocal(g_sum[:, 1, :], g_sum[:, 0, :]), b, 2)
                dve.tensor_tensor(g, g, g_sum[:, 1, :].unsqueeze(2).to_broadcast([P, EH, EK]), ALU.mult)\
                    .then_inc(pick_set, 1)
                assert n_step[0] == ROUTE_STEPS, n_step[0]
                dve.wait_ge(pickT_full, b + 1)
                dve.tensor_copy(i_T[:], ps[:, 6, 0:2 * P].rearrange("p (a t) -> p a t", a=2))
                dve.tensor_copy(g_hi[:], ps[:, 6, 2 * P:3 * P]).then_inc(pickT_set, 1)
                dve.wait_ge(pickT_set, 2 * b + 1)
                dve.tensor_tensor(g_lo[:], ps[:, 6, 2 * P:3 * P], g_hi[:].bitcast(F32), ALU.subtract)\
                    .then_inc(pickT_set, 1)
                dve.wait_ge(pickT_set, 2 * b + 2)
                dve.sem_inc(route_seen, 1)

            def settled2(ins, b, k):
                ins.then_inc(gsum_step, 1)
                dve.wait_ge(gsum_step, 2 * b + k)

            def mark(b, quad):
                q = 32 * b + quad
                tok = slice(4 * quad, 4 * quad + 4)
                keys = iota[:].unsqueeze(1).to_broadcast([P, 4, P])
                s = quad % 2
                dve.wait_ge(gate_full, q + 1)
                dve.tensor_tensor(match[:, s], keys, i_T[:, 1, tok].unsqueeze(2).to_broadcast([P, 4, P]),
                                  ALU.is_equal).then_inc(match_set, 1)
                dve.tensor_tensor(left[:, s], keys, i_T[:, 0, tok].unsqueeze(2).to_broadcast([P, 4, P]),
                                  ALU.is_equal).then_inc(left_set, 1)

            def add_low(b, quad):
                place = 4 * (quad % 8)
                four = stage[quad // 8 % 2][:, :, place:place + 4].rearrange("p j t -> p t j")
                dve.wait_ge(high_out, 32 * b + quad + 1)
                dve.tensor_tensor(four, gate_part(quad, 1), four, ALU.add).then_inc(gate_read, 1)

            dve.sem_inc(gate_read, 2)
            dve.wait_ge(sub_set, 16)
            with dve.Fori(0, NT) as b:
                route(b)
                for quad in range(P // 4 + 2):
                    if quad < P // 4:
                        mark(b, quad)
                    if quad >= 2:
                        add_low(b, quad - 2)

            def gate_times_gelu(j, k, m):
                slot = (k // 4) % 2
                if k % 4 == 0:
                    dve.wait_ge(gate_back[slot], m)
                    dve.wait_ge(gelu_back[slot], m)
                dve.tensor_tensor(gh[:, k % 2, :].rearrange("p (b t) -> p b t", b=NB),
                                  gate_in[slot][:, :, k % 4, :],
                                  gelu_in[slot][:, k % 4, :].rearrange("p (b t) -> p b t", b=NB), ALU.mult)\
                    .then_inc(gh_set, 1)
                dve.wait_ge(gh_hi_set, j + 1)
                dve.tensor_tensor(gh_lo[:, k % 4, :], gh[:, k % 2, :], gh_hi[:, k % 4, :].bitcast(F32),
                                  ALU.subtract).then_inc(gh_lo_set, 1)

            with dve.Fori(0, P // 8) as i:
                for k in range(8):
                    gate_times_gelu(8 * i + k, k, 16 * i + 16)
            ffn = ((ffn_full, U_END), var2_set, std2_set, norm2_set)
            dve.wait_ge(ln2_in, 32)
            for t in range(NT):
                norm(t, *ffn)
            last_tile(ln2_gt, ln2_bt, last_set)

        @block.tensor
        def _(pe):
            def three(out_, l_hi, l_lo, r_hi, r_lo, start, stop):
                pe.matmul(out_, l_hi, r_hi, start=start, stop=False)
                pe.matmul(out_, l_hi, r_lo, start=False, stop=False)
                return pe.matmul(out_, l_lo, r_hi, start=False, stop=stop)

            def project(n, bank, in_loop=0):
                pe.wait_ge(lo_done, in_loop + n + 1)
                s = n % RAW
                for c in range(KC):
                    if n == 0 and c % 2 == 0:
                        pe.wait_ge(x_lo, c // 2 + 1)
                    cols = slice(c * P, (c + 1) * P)
                    last = three(ps[:, bank, :], w_hi[:, s, cols], w_lo[:, s, cols], tok_hi[:, c, :], tok_lo[:, c, :],
                                 c == 0, c == KC - 1)
                last.then_inc(unit_done, 1)

            def att_unit(n):
                if n >= 2:
                    pe.wait_ge(bank_read, n - 1)
                project(n, n % 2)

            def tp_bank(what):
                i = plan[what][0]
                if i >= 2:
                    by, n = plan[i - 2]
                    pe.wait_ge(tp_read_act if by == "act" else tp_read_dve, n)
                return ps[:, 4 + i % 2, :]

            def v_to_tokens(n):
                bank = tp_bank(("v", n))
                pe.wait_ge(bank_read, n + 1)
                for t in range(NT):
                    last = pe.transpose(bank[:, t * P:(t + 1) * P], projT[:, V_UNITS[n][0], t * P:(t + 1) * P], ident[:])
                last.then_inc(tp_full, 1)

            def score_free(s):
                if s < 2:
                    return
                if s - 2 < 24:
                    pe.wait_ge(relu_done, s - 1)
                else:
                    pe.wait_ge(score_read, s - 2 - 24 + 1)

            def index_scores(first):
                pe.wait_ge(kidx_in, 4 * 16)
                for s in range(first, first + 4):
                    t, h = s // IH + 1, s % IH
                    rows = slice(ID * (h % 4), ID * (h % 4) + ID)
                    score_free(s)
                    pe.matmul(score_bank(s)[:, :(t + 1) * P], projT[rows, 6 + h // 4, t * P:(t + 1) * P],
                              projT[rows, 8, :(t + 1) * P], start=True, stop=True).then_inc(score_full, 1)

            def scores(u, half):
                kind, h = HEADS[u]
                pe.wait_ge(bank_read, QK_DONE[kind])
                if kind == "B":
                    rows, q_slot, k_slot = slice(HD * (h // 2), HD * (h // 2) + HD), h % 2, 2
                else:
                    rows, q_slot = slice(HD * (h % 2), HD * (h % 2) + HD), SET[kind] + h // 2
                    k_slot = SET[kind] + 2 + (0 if kind == "A" else h // 2)
                q, k = projT[rows, q_slot, :], projT[rows, k_slot, :]
                for i in (2 * half, 2 * half + 1):
                    s = 24 + 4 * u + i
                    score_free(s)
                    if kind == "D":
                        kt = keys_scored(u, i)
                        pe.matmul(score_bank(s)[:, :S - kt * P], k[:, kt * P:(kt + 1) * P], q[:, kt * P:S],
                                  start=True, stop=True).then_inc(score_full, 1)
                    else:
                        k0, n = keys_of(kind, i)
                        pe.matmul(score_bank(s)[:, :n], q[:, i * P:(i + 1) * P], k[:, k0:k0 + n],
                                  start=True, stop=True).then_inc(score_full, 1)

            def weights(u, half):
                kind, _ = HEADS[u]
                for i in (2 * half, 2 * half + 1):
                    bank = tp_bank(("u", u, i))
                    if kind == "D":
                        kt = keys_scored(u, i)
                        pe.wait_ge(softplus_set, 4 * (u - 4) + i + 1)
                        for k2 in range(kt, NT):
                            o, n = col_at(k2), S - k2 * P
                            last = pe.matmul(bank[:, (k2 - kt) * P:S - kt * P], (neg_after if k2 == kt else neg_ones)[:],
                                             row[u % 2][:, o:o + n], start=k2 == kt, stop=k2 == NT - 1)
                    else:
                        pe.wait_ge(probs_set, 4 * softmax_index(u) + 4)
                        for t in range(i, NT if kind != "B" else min(i + 2, NT)):
                            o = row_at(kind, t) + i * P - keys_of(kind, t)[0]
                            last = pe.transpose(bank[:, t * P:(t + 1) * P], row[u % 2][:, o:o + P], ident[:])
                    last.then_inc(tp_full, 1)

            def outputs(u):
                kind, h = HEADS[u]
                rows = slice(HD * (h % 2), HD * (h % 2) + HD)
                bank = ps[rows, 6 + (u // 2) % 2, :]
                if u >= 4 and u % 2 == 0:
                    pe.wait_ge(y_set, u // 2 - 1)
                if kind == "D":
                    pe.wait_ge(weight_exp, 4 * (u - 4) + 4)
                else:
                    pe.wait_ge(tp_read_act, plan["u", u, 3][2])
                chunk = V_CHUNK[kind] + (h // 2 if kind in "CD" else 0)
                c0 = {"A": 0, "B": HD * (h // 2)}.get(kind, HD * (h % 2))
                v = v_tok[:, chunk, :, c0:c0 + HD]
                if kind == "B":
                    for t in range(NT):
                        for kt in range(max(t - 1, 0), t + 1):
                            o = col_at(kt) + (t - kt) * P
                            last = pe.matmul(bank[:, t * P:(t + 1) * P], v[:, kt, :], colw[:, o:o + P],
                                             start=kt == max(t - 1, 0), stop=kt == t)
                else:
                    for kt in range(NT):
                        o, n = col_at(kt), S - kt * P
                        last = pe.matmul(bank[:, kt * P:S], v[:, kt, :], colw[:, o:o + n],
                                         start=kt == 0, stop=kt == NT - 1)
                last.then_inc(pv_done, 1)

            def branch(c, b):
                n = N_ATT + MERGE.index(("branch", c))
                pe.wait_ge(lo_done, n + 1)
                pe.wait_ge(y_lo_set, {2: 2, 3: 4, 1: 6, 0: 8}[b])
                if c == 0 and b in (2, 3):
                    pe.wait_ge(bank_read, N_ATT)
                elif c == 0:
                    pe.wait_ge(score_read, 4 * 16)
                elif c == 1 and b in (2, 3):
                    pe.wait_ge(tp_read_act, plan["u", 15, 3][2])
                elif c == 1:
                    pe.wait_ge(y_lo_set, 8)
                else:
                    pe.wait_ge(merge_step, 4 * c - (7 if c < NH else 3))
                for c2 in range(2):
                    g = 2 * b + c2
                    cols = slice(g * P, (g + 1) * P)
                    last = three(branch_bank(c, b), w_hi[:, n % RAW, cols], w_lo[:, n % RAW, cols],
                                 y_hi[g][:], y_lo[g][:], c2 == 0, c2 == 1)
                last.then_inc(unit_done if b == 0 else branch_full, 1)

            for n in range(N_FIRST):
                att_unit(n)
                if n == N_IDX:
                    pe.wait_ge(consts, 1)
                    v_to_tokens(2)
                if n >= N_IDX:
                    index_scores(4 * (n - N_IDX))
            v_to_tokens(7)
            v_to_tokens(8)
            for u in range(-1, 16):
                for half in range(2):
                    n = N_FIRST + 2 * u + half
                    if half == 0 and u >= 1:
                        outputs(u - 1)
                    if u + 1 < 16:
                        scores(u + 1, half)
                    if u >= 0:
                        weights(u, half)
                        if n < N_ATT:
                            att_unit(n)
                        if n - 1 in V_UNITS and n - 1 >= N_FIRST:
                            v_to_tokens(n - 1)
                    for b in {(14, 1): (2, 3), (15, 1): (1,)}.get((u, half), ()):
                        branch(0, b)
            outputs(15)
            branch(1, 2)
            branch(1, 3)
            branch(0, 0)

            late = 0
            for k, (kind, c) in enumerate(MERGE):
                n = N_ATT + k
                if kind == "gate":
                    pe.wait_ge(bank_read, max(N_ATT + late - 1, N_ATT))
                    if late < 2:
                        pe.wait_ge(merge_step, 4 * 2 + 1)
                    project(n, late % 2)
                    late += 1
                    continue
                for b in {0: (), 1: (1, 0)}.get(c, (2, 3, 1, 0)):
                    branch(c, b)

            def add_tile(n, t, l_hi, l_lo, start, stop):
                s = n % RAW
                tile_ = slice(t * P, (t + 1) * P)
                h = [(ps[:, 2 * t + a, :], w_hi[:, s, a * S:a * S + S], w_lo[:, s, a * S:a * S + S]) for a in range(2)]
                for o, wh, wl in h:
                    pe.matmul(o, l_hi[:, tile_], wh, start=start, stop=False)
                    pe.matmul(o, l_hi[:, tile_], wl, start=False, stop=False)
                for o, wh, wl in h:
                    last = pe.matmul(o, l_lo[:, tile_], wh, start=False, stop=stop)
                return last

            def last_units(first, ready, operands, full, between):
                for t in range(NT):
                    for k in range(RAW):
                        n = first + k
                        if t == 0:
                            pe.wait_ge(lo_done, n + 1)
                            ready(k)
                        last = add_tile(n, t, *operands(k), False, k == RAW - 1)
                        if t == NT - 1:
                            last.then_inc(unit_done, 1)
                        between(t, k)
                    if t < NT - 1:
                        last.then_inc(full, 1)

            def transpose_h(t):
                pe.wait_ge(h_set, t + 1)
                for c in range(KC):
                    last = pe.transpose(ps[:, 2 * t + c // 4, (c % 4) * P:(c % 4 + 1) * P],
                                        x_tok[:, t, c * P:(c + 1) * P], ident[:])
                last.then_inc(hT_full, 1)

            def project_half(n, bank, half):
                if half == 0:
                    pe.wait_ge(lo_done, n + 1)
                tokens = slice(half * S // 2, (half + 1) * S // 2)
                for c in range(KC):
                    cols = slice(c * P, (c + 1) * P)
                    last = three(ps[:, bank, tokens], w_hi[:, n % RAW, cols], w_lo[:, n % RAW, cols],
                                 tok_hi[:, c, tokens], tok_lo[:, c, tokens], c == 0, c == KC - 1)
                if half == 1:
                    last.then_inc(unit_done, 1)

            pe.wait_ge(bank_read, N_ATT + 16)
            for c in range(RAW):
                pe.wait_ge(lo_done, U_OUT + c + 1)
                pe.wait_ge(m_set, c + 1)
                for t in ((0, 3, 1, 2) if c == 0 else range(NT)):
                    if c == 0 and t == 1:
                        pe.wait_ge(merge_step, 4 * (KC - 1) + 1)
                    last = add_tile(U_OUT + c, t, m_hi[:, c, :], m_lo[:, c, :], c == 0, False)
                last.then_inc(unit_done, 1)
            last_units(U_OUT + RAW, lambda k: pe.wait_ge(m_set, RAW + k + 1),
                       lambda k: (m_hi[:, RAW + k, :], m_lo[:, RAW + k, :]), mix_full,
                       lambda t, k: transpose_h(0) if (t, k) == (3, 1) else None)
            transpose_h(1)
            pe.wait_ge(hT_lo, 2)
            for k in range(RAW):
                project_half(U_WQ + k, k, 0)
                if k in (1, 2):
                    transpose_h(k + 1)
            pe.wait_ge(hT_lo, NT)
            for k in range(RAW):
                project_half(U_WQ + k, k, 1)
            for h in range(RAW, EH):
                project(U_WQ + h, h)
            pe.wait_ge(q_lo_set, 1)
            project(U_EXP, 0)
            pe.wait_ge(sk_lo_set, 1)
            pe.wait_ge(q_lo_set, EH)
            for f in range(16):
                t = f // 4
                if f >= 4:
                    pe.wait_ge(sub_set, f - 3)
                for a in range(2):
                    h = 2 * (f % 4) + a
                    tile_ = slice(t * P, (t + 1) * P)
                    last = three(ps[:, 2 + f % 4, 2 * NK * a:2 * NK * a + 2 * NK], q_hi[:, h, tile_], q_lo[:, h, tile_],
                                 sk_hi[:, h, :], sk_lo[:, h, :], True, True)
                last.then_inc(sub_full, 1)

            def expert_unit(j, in_loop, first=False):
                if not first:
                    pe.wait_ge(bank_read, in_loop + BANK_EXP + j - 1)
                project(U_EXP + j, j % 2, in_loop)

            pe.sem_inc(gate_full, 2)
            for k in range(1, 4):
                expert_unit(k, 0, first=k < 2)
            with pe.Fori(0, ROUTE_UNITS // 4 - 1) as i:
                for k in range(4):
                    expert_unit(4 + k, 4 * i)
            pe.wait_ge(sub_set, 16)
            with pe.Fori(0, NT) as b:
                for k in range(8):
                    expert_unit(ROUTE_UNITS + k, 28 * b)
                pe.wait_ge(pick_set, b + 1)
                for k in range(3):
                    last = pe.transpose(ps[:, 6, k * P:(k + 1) * P], pick[:, k, :], ident[:])
                last.then_inc(pickT_full, 1)
                with pe.Fori(0, 2) as i:
                    for body in range(2):
                        for k in range(4):
                            expert_unit(ROUTE_UNITS + 8 + 4 * body + k, 28 * b + 8 * i)
                            for quad in (2 * k, 2 * k + 1):
                                q = 32 * b + 16 * i + 8 * body + quad
                                s = quad % 2
                                pe.wait_ge(left_set, q + 1)
                                pe.wait_ge(right_set, q + 1)
                                pe.wait_ge(right_lo_set, q + 1)
                                pe.wait_ge(gate_read, q + 1)
                                for t in range(4):
                                    last = pe.matmul(ps[:, 2 + 2 * s + t // 2, (t % 2) * 2 * P:(t % 2 + 1) * 2 * P],
                                                     left[:, s, t], right[:, s, t].rearrange("p a j -> p (a j)"),
                                                     start=True, stop=True)
                                last.then_inc(gate_full, 1)
                for k in range(4):
                    expert_unit(ROUTE_UNITS + 24 + k, 28 * b)
            for k in range(4):
                expert_unit(124 + k, 0)

            def value_unit(j, in_loop, start=False):
                n = U_VAL + j
                pe.wait_ge(lo_done, in_loop + n + 1)
                pe.wait_ge(gh_lo_set, in_loop + j + 1)
                for t in ((3, 2, 1, 0) if start else range(NT)):
                    if start and t == 0:
                        pe.wait_ge(bank_read, BANK_EXP + P)
                    last = add_tile(n, t, gh_hi[:, j % 4, :], gh_lo[:, j % 4, :], start, False)
                last.then_inc(unit_done, 1)

            pe.wait_ge(gate_read, 2 + P)
            for k in range(4):
                value_unit(k, 0, start=k == 0)
            with pe.Fori(0, P // 4 - 2) as i:
                for k in range(4):
                    value_unit(4 + k, 4 * i)
            last_units(U_END - RAW, lambda k: pe.wait_ge(gh_lo_set, P - RAW + k + 1),
                       lambda k: (gh_hi[:, k, :], gh_lo[:, k, :]), ffn_full, lambda t, k: None)


def _unit(w):
    return w.reshape(KC, P, P).transpose(1, 0, 2).reshape(P, DM)


def kernel(x, w_in, w_branch, w_out, attn_sinks, ln1_g, ln1_b, peer_wq, peer_subkeys,
           peer_u, peer_v, ln2_g, ln2_b):
    import numpy as np
    import concourse.bacc as bacc
    from concourse.bass_utils import run_bass_kernel_spmd

    a = {k: np.asarray(v) for k, v in dict(
        x=x, w_in=w_in, w_branch=w_branch, w_out=w_out, sinks=attn_sinks, ln1_g=ln1_g, ln1_b=ln1_b,
        wq=peer_wq, subk=peer_subkeys, u=peer_u, v=peer_v, ln2_g=ln2_g, ln2_b=ln2_b).items()}
    names = ["qa", "ka", "va", "qi", "ki", "wi", "qb", "kb", "vb", "qc", "kc", "vc", "qd", "kd", "vd", "g"]
    widths = [256, 64, 64, 256, 32, 8, 256, 128, 128, 256, 256, 256, 256, 256, 256, 4 * DM]
    ends = np.cumsum(widths)
    w = {n: a["w_in"][0][:, e - m:e] for n, m, e in zip(names, widths, ends)}

    def two(n):
        return [w[n][:, :P], w[n][:, P:]]

    cat = lambda *p: np.concatenate(p, axis=1)
    gate = [w["g"][:, (g % 4) * DM + (g // 4) * P:(g % 4) * DM + (g // 4) * P + P] for g in range(32)]
    qb = w["qb"].reshape(DM, 2, 2, HD).transpose(0, 2, 1, 3).reshape(DM, 256)
    proj = two("qi") + [cat(w["va"], w["ki"], w["wi"], w["va"][:, :24])] + \
        two("qc") + two("kc") + two("vc") + two("qd") + two("kd") + two("vd") + \
        [qb[:, :P], qb[:, P:], w["kb"], w["vb"]] + two("qa") + [cat(w["ka"], w["ka"])]
    proj, units = iter(proj), []
    for kind, k in UNITS:
        units.append(_unit(next(proj) if kind == "proj" else gate[k]))
    for kind, c in MERGE:
        if kind == "gate":
            units.append(_unit(gate[c]))
        else:
            b = a["w_branch"][0][:, :, c * P:(c + 1) * P].reshape(8, P, P)
            units.append(b.transpose(1, 0, 2).reshape(P, DM))
    units += list(a["w_out"][0].reshape(KC, P, DM))
    units += [_unit(a["wq"][0][:, h * P:(h + 1) * P]) for h in range(EH)]
    rows = a["x"].reshape(S, DM)
    arrays = {
        "xT": rows.T.reshape(KC, P, S).transpose(1, 0, 2),
        "x_rows": rows,
        "w_units": np.stack(units),
        "u_units": a["u"][0].reshape(P, P, KC, P).transpose(1, 3, 2, 0).reshape(P, P, DM),
        "v_rows": a["v"][0].reshape(P, P, DM),
        "sinks": a["sinks"].reshape(1, NH),
        "ln1_g": a["ln1_g"].reshape(1, DM), "ln1_b": a["ln1_b"].reshape(1, DM),
        "subk": a["subk"][0].transpose(1, 3, 0, 2),
        "ln2_g": a["ln2_g"].reshape(1, DM), "ln2_b": a["ln2_b"].reshape(1, DM),
    }
    arrays = {k: np.ascontiguousarray(v) for k, v in arrays.items()}
    nc = bacc.Bacc("TRN2", target_bir_lowering=False, num_devices=1)
    args = [nc.dram_tensor(k, v.shape, F32, kind="ExternalInput").ap() for k, v in arrays.items()]
    args.append(nc.dram_tensor("gelu_d", (P, P, S), F32, kind="Internal").ap())
    args.append(nc.dram_tensor("gate_d", (NB, P, P, TOK), F32, kind="Internal").ap())
    args.append(nc.dram_tensor("out", (S, DM), F32, kind="ExternalOutput").ap())
    peer_block(nc, *args)
    r = run_bass_kernel_spmd(nc, [arrays], core_ids=[0])
    return r.results[0]["out"].reshape(1, S, DM)
```
